# Optimizing a Trainium2 kernel written in Bass

```python
import jax, jax.numpy as jnp
from jax import lax
import numpy as np

D_MODEL = 1024
BATCH = 1
SEQ = 256
DEPTH = 1

HEAD_DIM = 64
ATT_GROUPS = ((128, 1), (512, 4), (2048, 16))
N_DIL = len(ATT_GROUPS)
HEADS_PER_GROUP = 4
N_ATT_HEADS = N_DIL * HEADS_PER_GROUP
ATT_W = N_ATT_HEADS * HEAD_DIM
ATT_OUT_W = HEADS_PER_GROUP * HEAD_DIM
BLK = 128
REL_BUCKETS = 32
REL_MAX_DIST = 2048
CHUNK = 128
GMLP_W = 768
GMLP_GROUPS = 12
GMLP_GD = GMLP_W // GMLP_GROUPS
N_BRANCH = 2
IN_W = 3 * ATT_W + 2 * GMLP_W + N_BRANCH * D_MODEL
N_EXPERTS = 32
TOP_K = 4
D_EXPERT = D_MODEL
SWIGLU_LIMIT = 7.0
SWIGLU_ALPHA = 1.702
MOE_BLK = 128
PLE_DIM = 256
EPS = 1e-6

kernel_name = "hybrid_dilated_gmlp_moe_block"

def _rmsnorm(x, g):
    xf = x.astype(jnp.float32)
    y = xf * lax.rsqrt(jnp.mean(xf * xf, axis=-1, keepdims=True) + EPS) * g.astype(jnp.float32)
    return y.astype(x.dtype)

def _t5_bucket(n):
    exact = REL_BUCKETS // 2
    nf = np.maximum(n, 1).astype(np.float32)
    large = exact + (np.log(nf / exact) / np.log(REL_MAX_DIST / exact) * (REL_BUCKETS - exact)).astype(np.int32)
    large = np.minimum(large, REL_BUCKETS - 1)
    return np.where(n < exact, n, large).astype(np.int32)

def _dilated_group(q, k, v, rel_bias_g, window, dilation):
    B, S, H, E = q.shape
    span = window // dilation
    unit = dilation * BLK
    Sp = -(-S // unit) * unit
    nb = Sp // unit

    def to_blocks(t):
        t = jnp.pad(t, ((0, 0), (0, Sp - S), (0, 0), (0, 0)))
        return t.reshape(B, nb, BLK, dilation, H, E)

    qb, kb, vb = to_blocks(q), to_blocks(k), to_blocks(v)

    def with_prev(t):
        prev = jnp.pad(t, ((0, 0), (1, 0), (0, 0), (0, 0), (0, 0), (0, 0)))[:, :-1]
        return jnp.concatenate([prev, t], axis=2)

    kk, vv = with_prev(kb), with_prev(vb)

    i = np.arange(BLK)[:, None]
    j = np.arange(2 * BLK)[None, :]
    dist = i + BLK - j
    band = (dist >= 0) & (dist <= span)
    bucket = _t5_bucket(np.clip(dist, 0, None) * dilation)
    bias = jnp.transpose(rel_bias_g[bucket], (2, 0, 1)).astype(jnp.float32)
    key_ok = (np.arange(nb)[:, None] * BLK + np.arange(2 * BLK)[None, :] - BLK) >= 0
    mask = jnp.asarray(band[None, :, :] & key_ok[:, None, :])

    logits = jnp.einsum('bnqrhe,bnkrhe->bnrhqk', qb, kk).astype(jnp.float32) * (E ** -0.5)
    logits = logits + bias[None, None, None]
    logits = jnp.where(mask[None, :, None, None], logits, -jnp.inf)
    m = jnp.max(logits, axis=-1, keepdims=True)
    w = jnp.exp(logits - m)
    den = jnp.sum(w, axis=-1)
    num = jnp.einsum('bnrhqk,bnkrhe->bnqrhe', w.astype(vv.dtype), vv).astype(jnp.float32)
    den_t = jnp.transpose(den, (0, 1, 4, 2, 3))
    lse = jnp.transpose(m[..., 0] + jnp.log(den), (0, 1, 4, 2, 3))
    out = (num / den_t[..., None]).reshape(B, Sp, H, E)[:, :S]
    lse = lse.reshape(B, Sp, H)[:, :S]
    return out, lse

def _dilated_attention(q, k, v, rel_bias):
    outs, lses = [], []
    for g, (window, dilation) in enumerate(ATT_GROUPS):
        o, l = _dilated_group(q[:, :, g], k[:, :, g], v[:, :, g],
                              rel_bias[:, g * HEADS_PER_GROUP:(g + 1) * HEADS_PER_GROUP], window, dilation)
        outs.append(o)
        lses.append(l)
    outs = jnp.stack(outs, axis=2)
    alpha = jax.nn.softmax(jnp.stack(lses, axis=2), axis=2)
    return jnp.sum(alpha[..., None] * outs, axis=2)

def _spatial_gating(u_raw, v_raw, ln_g, ln_b, w_s, b_s):
    B, S, _ = u_raw.shape
    zu = jax.nn.gelu(u_raw, approximate=False)
    zv = jax.nn.gelu(v_raw, approximate=False).astype(jnp.float32)
    mu = jnp.mean(zv, axis=-1, keepdims=True)
    var = jnp.mean(jnp.square(zv - mu), axis=-1, keepdims=True)
    vn = (zv - mu) * lax.rsqrt(var + EPS) * ln_g.astype(jnp.float32) + ln_b.astype(jnp.float32)
    vc = vn.reshape(B, S // CHUNK, CHUNK, GMLP_GROUPS, GMLP_GD)
    causal = jnp.asarray(np.tril(np.ones((CHUNK, CHUNK), np.float32)))
    w_c = w_s.astype(jnp.float32) * causal[None]
    mixed = jnp.einsum('gij,bcjgd->bcigd', w_c, vc) + b_s.astype(jnp.float32).T[None, None, :, :, None]
    return zu * mixed.reshape(B, S, GMLP_W).astype(zu.dtype)

def _moe(hn, w_router, b_router, w_gate_up, b_gate_up, w_down, b_down):
    B, S, D = hn.shape
    T = B * S
    xt = hn.reshape(T, D)
    logits = (xt @ w_router + b_router).astype(jnp.float32)
    top_val, top_idx = lax.top_k(logits, TOP_K)
    gate = jax.nn.softmax(top_val, axis=-1)
    A = T * TOP_K
    flat_e = top_idx.reshape(A).astype(jnp.int32)
    flat_tok = jnp.repeat(jnp.arange(T, dtype=jnp.int32), TOP_K)
    flat_gate = gate.reshape(A)
    order = jnp.argsort(flat_e)
    e_sorted = flat_e[order]
    counts = jnp.bincount(flat_e, length=N_EXPERTS).astype(jnp.int32)
    start = jnp.cumsum(counts) - counts
    blk_counts = (counts + MOE_BLK - 1) // MOE_BLK
    blk_end = jnp.cumsum(blk_counts)
    pad_start = (blk_end - blk_counts) * MOE_BLK
    rank = jnp.arange(A, dtype=jnp.int32) - start[e_sorted]
    dest = pad_start[e_sorted] + rank
    n_blocks = -(-A // MOE_BLK) + N_EXPERTS
    P = n_blocks * MOE_BLK
    slot_tok = jnp.full((P,), T, jnp.int32).at[dest].set(flat_tok[order])
    slot_gate = jnp.zeros((P,), jnp.float32).at[dest].set(flat_gate[order])
    block_expert = jnp.minimum(
        jnp.searchsorted(blk_end, jnp.arange(n_blocks, dtype=jnp.int32), side='right'), N_EXPERTS - 1)
    x_pad = jnp.concatenate([xt, jnp.zeros((1, D), xt.dtype)], axis=0)
    xb = x_pad[slot_tok].reshape(n_blocks, MOE_BLK, D)

    def expert_block(args):
        xe, e = args
        gu = xe @ w_gate_up[e] + b_gate_up[e]
        glu = jnp.minimum(gu[:, :D_EXPERT], SWIGLU_LIMIT)
        lin = jnp.clip(gu[:, D_EXPERT:], -SWIGLU_LIMIT, SWIGLU_LIMIT)
        act = glu * jax.nn.sigmoid(SWIGLU_ALPHA * glu) * (lin + 1.0)
        return act @ w_down[e] + b_down[e]

    yb = lax.map(expert_block, (xb, block_expert))
    y = yb.reshape(P, D) * slot_gate[:, None].astype(yb.dtype)
    out = jnp.zeros((T + 1, D), yb.dtype).at[slot_tok].add(y)[:T]
    return out.reshape(B, S, D)

def setup_inputs(seed: int = 0) -> dict:
    key = jax.random.key(seed)
    ks = jax.random.split(key, 24)
    f32 = jnp.float32
    nrm = lambda k, shape, s: jax.random.normal(k, shape, f32) * s
    L, D, E = DEPTH, D_MODEL, N_EXPERTS
    return {
        "x": nrm(ks[0], (BATCH, SEQ, D), 1.0),
        "p": nrm(ks[1], (DEPTH, BATCH, SEQ, PLE_DIM), 1.0),
        "g_mix": 1.0 + nrm(ks[2], (L, D), 0.05),
        "w_in": nrm(ks[3], (L, D, IN_W), D ** -0.5),
        "rel_bias": nrm(ks[4], (REL_BUCKETS, N_ATT_HEADS), 0.5),
        "w_att_out": nrm(ks[5], (L, ATT_OUT_W, D), ATT_OUT_W ** -0.5),
        "ln_v_g": 1.0 + nrm(ks[6], (L, GMLP_W), 0.05),
        "ln_v_b": nrm(ks[7], (L, GMLP_W), 0.02),
        "w_spatial": nrm(ks[8], (L, GMLP_GROUPS, CHUNK, CHUNK), CHUNK ** -0.5),
        "b_spatial": 1.0 + nrm(ks[9], (L, GMLP_GROUPS, CHUNK), 0.1),
        "w_gmlp_out": nrm(ks[10], (L, GMLP_W, D), GMLP_W ** -0.5),
        "w_out": nrm(ks[11], (L, D, D), D ** -0.5),
        "g_moe": 1.0 + nrm(ks[12], (L, D), 0.05),
        "w_router": nrm(ks[13], (L, D, E), D ** -0.5),
        "b_router": nrm(ks[14], (L, E), 0.01),
        "w_gate_up": nrm(ks[15], (L, E, D, 2 * D_EXPERT), D ** -0.5),
        "b_gate_up": nrm(ks[16], (L, E, 2 * D_EXPERT), 0.02),
        "w_down": nrm(ks[17], (L, E, D_EXPERT, D), D_EXPERT ** -0.5),
        "b_down": nrm(ks[18], (L, E, D), 0.02),
        "g_ple": 1.0 + nrm(ks[19], (L, D), 0.05),
        "w_ple_gate": nrm(ks[20], (L, D, D), D ** -0.5),
        "w_ple_proj": nrm(ks[21], (L, PLE_DIM, D), PLE_DIM ** -0.5),
        "g_final": 1.0 + nrm(ks[22], (D,), 0.05),
    }

def reference(x, p, g_mix, w_in, rel_bias, w_att_out, ln_v_g, ln_v_b, w_spatial, b_spatial,
              w_gmlp_out, w_out, g_moe, w_router, b_router, w_gate_up, b_gate_up, w_down, b_down,
              g_ple, w_ple_gate, w_ple_proj, g_final):
    B, S, D = x.shape
    splits = [int(c) for c in np.cumsum([ATT_W, ATT_W, ATT_W, GMLP_W, GMLP_W])]
    h = x
    for i in range(DEPTH):
        n1 = _rmsnorm(h, g_mix[i])
        z = n1 @ w_in[i]
        q, k, v, u_raw, v_raw, gate_logits = jnp.split(z, splits, axis=-1)
        hs = (B, S, N_DIL, HEADS_PER_GROUP, HEAD_DIM)
        att = _dilated_attention(q.reshape(hs), k.reshape(hs), v.reshape(hs), rel_bias)
        y_att = att.reshape(B, S, ATT_OUT_W).astype(h.dtype) @ w_att_out[i]
        y_gm = _spatial_gating(u_raw, v_raw, ln_v_g[i], ln_v_b[i], w_spatial[i], b_spatial[i]) @ w_gmlp_out[i]
        gates = jax.nn.sigmoid(gate_logits.reshape(B, S, N_BRANCH, D))
        merged = gates[:, :, 0] * y_att + gates[:, :, 1] * y_gm
        h = h + merged @ w_out[i]
        h = h + _moe(_rmsnorm(h, g_moe[i]), w_router[i], b_router[i], w_gate_up[i], b_gate_up[i],
                     w_down[i], b_down[i])
        ple_gate = jax.nn.sigmoid(_rmsnorm(h, g_ple[i]) @ w_ple_gate[i])
        h = h + ple_gate * (p[i] @ w_ple_proj[i])
    return _rmsnorm(h, g_final)


_drawn_inputs = setup_inputs


def setup_inputs(seed=0):
    import zlib

    import numpy as np

    out = dict(_drawn_inputs(seed))
    spreads = {}
    factors = {'ln_v_b': 3.908, 'b_gate_up': 5.944, 'b_down': 6.866, 'g_ple': 7.119}
    for name, (base, spread) in spreads.items():
        noise = np.random.default_rng([zlib.crc32(name.encode()), seed]).standard_normal(out[name].shape)
        drawn = base * np.exp(spread * noise) if base else spread * noise
        out[name] = __import__('jax').numpy.asarray(drawn.astype(out[name].dtype))
    for name, factor in factors.items():
        out[name] = (out[name] * factor).astype(out[name].dtype)
    return out
```

```python
from contextlib import ExitStack

import concourse.bass as bass
import concourse.mybir as mybir

F32 = mybir.dt.float32
BF16 = mybir.dt.bfloat16
I32 = mybir.dt.int32
U32 = mybir.dt.uint32
ALU = mybir.AluOpType
ACT = mybir.ActivationFunctionType
AX = mybir.AxisListType

P = 128
D = 1024
KC = D // P
TB = 2
T = TB * P
HD = 64
SLOTS_PER_GROUP = 4
GROUPS = 3
HEADS = GROUPS * SLOTS_PER_GROUP
QKV = HEADS * HD
GM = 768
GMG = 12
UV0 = 3 * QKV
GATE0 = UV0 + 2 * GM
BLKN = 512
NB = D // BLKN
E = 32
TOP = 4
CAP = 64
PAIRS = E // 2
PASSES = T // CAP
BUCKETS = 32
SKEW = 384
EPS = 1e-6
BF16_ONE = 0x3F80
LIMIT = 7.0
ALPHA = 1.702
SLOT = 4096
RING = 8
EARLY = 6
ORDER = [0, 1, 2, 5, 6, 7, 3, 4]
LOADS = 12
UPL = 4
IDENT, TRIL, BEFORE, IOTA, CONSTS = 0, 128, 256, 384, 448


def in_widths():
    return [BLKN] * 4 + [QKV - BLKN] + [BLKN] * 7


def build(nc, ctx, a, out):
    def sb(name, shape, dt=F32):
        return ctx.enter_context(nc.sbuf_tensor(name, shape, dt))

    def sem(name):
        return ctx.enter_context(nc.semaphore(name))

    ring = sb("ring", [P, RING, SLOT])
    h = sb("h", [P, TB, D])
    xn = sb("xn", [P, TB, D])
    xt = sb("xt", [P, 2 * D])
    stage = sb("stage", [P, 3 * D])
    work = sb("work", [P, 3 * D])
    late = sb("late", [P, 1536])
    bias_gu = sb("bias_gu", [3 * E, 2 * D], BF16)
    pick = sb("pick", [3 * E, PAIRS * P], BF16)
    bdown = sb("bdown", [E, D])
    pT = sb("pT", [P, 2, T])
    gain = sb("gain", [P, D])
    const = sb("const", [P, CONSTS])
    wr = sb("wr", [P, KC, E])
    rank_of = sb("rank_of", [P, TB, PASSES * E + 4])
    gate_of = sb("gate_of", [P, TB, PASSES * E + 4])
    cols = sb("cols", [P, 2, KC])
    bs = sb("bs", [P, GMG])
    ones = sb("ones", [P, P])
    tiny = sb("tiny", [P, 96])
    route = sb("route", [P, 96])
    count = sb("count", [P, 1], I32)
    top_i = sb("top_i", [P, TB, 8], U32)
    ps = ctx.enter_context(nc.psum_tensor("ps", [P, 8, BLKN], F32))

    ident = const[:, IDENT:IDENT + P]
    before = const[:, BEFORE:BEFORE + P]
    tril_t = const[:, TRIL:TRIL + P]
    iota = const[:, IOTA:IOTA + CAP]
    xt_all = xt[:, :].rearrange("p (c t) -> p c t", c=KC)
    xt_tb = xt[:, :].rearrange("p (b c t) -> p b c t", b=TB, c=KC)
    scratch = ring[:, EARLY:RING, :].rearrange("p s n -> p (s n)")
    btab = scratch[:, 0:HEADS * T].rearrange("p (h s) -> p h s", h=HEADS)
    qkT = scratch[:, 3072:6144].rearrange("p (c t) -> p c t", c=12)
    vsb = scratch[:, 6144:7680].rearrange("p (b n) -> p b n", b=TB)
    attT = scratch[:, 7680:8192].rearrange("p (c t) -> p c t", c=2)
    gT = scratch[:, 0:1536].rearrange("p (c t) -> p c t", c=6)
    prob = stage[:, 0:1536].rearrange("p (b g s) -> p b g s", b=2, g=GROUPS)
    probT = stage[:, 1536:2304]
    sig = stage[:, 1024:2048].rearrange("p (b n) -> p b n", b=2)
    gated = stage[:, 2048:2560]
    ws_raw = stage[:, 0:1536].rearrange("p (g j) -> p g j", g=GMG)
    vals = stage[0:SLOTS_PER_GROUP, 1536:1536 + GROUPS * SKEW].rearrange("p (g u) -> p g u", g=GROUPS)
    xt_route = stage[:, 0:2048].rearrange("p (b c t) -> p b c t", b=TB, c=KC)
    raw_bgu = work[0:3 * E, 0:2 * D]
    uv = work[:, :].rearrange("p (b n) -> p b n", b=TB)
    onehot = late[0:BUCKETS + 1, 0:GROUPS * SKEW].rearrange("p (g u) -> p g u", g=GROUPS)
    wsT = late[:, :].rearrange("p (g i) -> p g i", g=GMG)
    lng, lnb = xn[:, 0, 0:GM], xn[:, 1, 0:GM]
    relb = tiny[0:BUCKETS + 1, 80:92]
    act = stage[:, 0:D]
    actT = stage[:, D:2 * D].rearrange("p (c t) -> p c t", c=KC)
    ysb = stage[:, 2 * D:3 * D]
    glu = work[:, 0:D].rearrange("p (b n) -> p b n", b=2)
    sigm = work[:, D:2 * D].rearrange("p (b n) -> p b n", b=2)
    lin = work[:, 2 * D:3 * D].rearrange("p (b n) -> p b n", b=2)
    sel = late[:, 0:512].rearrange("p (q b s) -> p q b s", q=2, b=TB)
    selg = late[:, 512:1024].rearrange("p (q b s) -> p q b s", q=2, b=TB)
    selgT = late[:, 1024:1280].rearrange("p (b t) -> p b t", b=TB)
    mean_sq, rstd = tiny[:, 0:8], tiny[:, 8:16]
    row_max, neg_max, den, rden = tiny[:, 16:24], tiny[:, 24:32], tiny[:, 32:40], tiny[:, 40:48]
    ln_sum, ln_nm, ln_ss, ln_var, ln_rstd = (tiny[:, 48 + 2 * k:50 + 2 * k] for k in range(5))
    rms_var = tiny[:, 64:72]
    half = tiny[:, 72:73]
    fullest, passes = tiny[:, 58:59], tiny[:, 59:63]
    top_v = route[:, 0:16].rearrange("p (b k) -> p b k", b=TB)
    top_e = route[:, 16:24].rearrange("p (b k) -> p b k", b=TB)
    top_s, top_r = route[:, 24:26], route[:, 26:28]
    top_g = route[:, 32:40].rearrange("p (b k) -> p b k", b=TB)
    brout = route[:, 40:72]
    logits = work[:, 0:64].rearrange("p (b e) -> p b e", b=TB)
    chosen = work[:, 64:320].rearrange("p (b k e) -> p b k e", b=TB, k=TOP)
    weighted = work[:, 320:576].rearrange("p (b k e) -> p b k e", b=TB, k=TOP)
    mask = work[:, 576:640].rearrange("p (b e) -> p b e", b=TB)
    gates = work[:, 640:704].rearrange("p (b e) -> p b e", b=TB)
    rank1 = work[:, 704:768].rearrange("p (b e) -> p b e", b=TB)
    gatesT = work[0:E, 768:1024].rearrange("p (b t) -> p b t", b=TB)

    skewed = nc.dram_tensor("skewed", [HEADS, P, SKEW], F32)

    def bank(k, n=1):
        return ps[:, k:k + n, :].rearrange("p b n -> p (b n)")

    w_out = a["w_out"][0].rearrange("(p c) n -> p c n", c=KC)
    w_gm = a["w_gmlp_out"][0].rearrange("(c p) n -> p c n", p=P)
    widths = in_widths()

    def w_in(k):
        c0 = sum(widths[:k])
        return a["w_in"][:, KC * c0:KC * (c0 + widths[k])].rearrange("p (c n) -> p c n", c=KC)

    early_views = [w_in(k) for k in range(10)]
    early_views += [a["w_att_out"][0].rearrange("(c p) n -> p c n", p=P)]
    early_views += [w_in(10), w_in(11)]
    early_views += [w_gm[:, 0:3, :], w_gm[:, 3:6, :], w_out[:, 0:4, :], w_out[:, 4:8, :]]
    (L_QK, L_V, L_UV, L_GA, L_ATT, L_GB, L_GM, L_WO) = (0, 3, 5, 8, 10, 11, 13, 15)
    n_early = len(early_views)

    def early_slot(k):
        c, n = early_views[k].shape[1:]
        return ring[:, k % EARLY, 0:c * n].rearrange("p (c n) -> p c n", c=c)

    w_up = a["w_gate_up"][0].rearrange("e (p c) n -> e p (c n)", c=KC)
    w_dn = a["w_down"][0].rearrange("e (p c) n -> e p (c n)", c=KC)
    w_pp = a["w_ple_proj"][0].rearrange("(p c) n -> p c n", c=2)
    w_pg = a["w_ple_gate"][0].rearrange("(p c) n -> p (c n)", c=KC)

    x_in, const_in, bgu_in, ws_in, small_in, ln_in, gmoe_in, gfin_in, bdown_in, rel_in, skew_out, btab_in = (
        sem(n) for n in ("x_in", "const_in", "bgu_in", "ws_in", "small_in", "ln_in", "gmoe_in", "gfin_in",
                         "bdown_in", "rel_in", "skew_out", "btab_in"))
    early_in = [sem(f"early_in{k}") for k in range(EARLY)]
    moe_in = [sem(f"moe_in{k}") for k in range(RING)]
    moe_free = sem("moe_free")
    ple_in = [sem(f"ple_in{k}") for k in range(3)]
    dve_step, act_step = sem("dve_step"), sem("act_step")
    ones_ready, bgu_ready, merged_ready = sem("ones_ready"), sem("bgu_ready"), sem("merged_ready")
    vals_done, vals_ready = sem("vals_done"), sem("vals_ready")
    sq_done, xn_ready, xT_done, xT_ready = sem("sq_done"), sem("xn_ready"), sem("xT_done"), sem("xT_ready")
    xT_ready2 = sem("xT_ready2")
    ws_ready = sem("ws_ready")
    proj_done, proj_free = sem("proj_done"), sem("proj_free")
    qk_done, qk_read, nm_ready, exp_done, prob_ready = (
        sem(n) for n in ("qk_done", "qk_read", "nm_ready", "exp_done", "prob_ready"))
    pT_done, pT_ready, pv_done, att_ready = sem("pT_done"), sem("pT_ready"), sem("pv_done"), sem("att_ready")
    gelu_done, vn_ready, mixed_done, mixed_read, g_ready, gT_done, gT_ready = (
        sem(n) for n in ("gelu_done", "vn_ready", "mixed_done", "mixed_read", "g_ready", "gT_done", "gT_ready"))
    y_done, y_read = sem("y_done"), sem("y_read")
    mT_done, mT_ready, wo_done, h_ready = sem("mT_done"), sem("mT_ready"), sem("wo_done"), sem("h_ready")
    rt_done, mask_ready, top_sub, top_exp, gates_ready, rank_done, gatesT_done, gatesT_ready = (
        sem(n) for n in ("rt_done", "mask_ready", "top_sub", "top_exp", "gates_ready", "rank_done", "gatesT_done",
                         "gatesT_ready"))
    bd_done, count_ready = sem("bd_done"), sem("count_ready")
    sel_ready, xg_done, xg_ready = sem("sel_ready"), sem("xg_done"), sem("xg_ready")
    gu_half, glu_ready, sig_ready, lin_ready, mix_ready, act_ready = (
        sem(n) for n in ("gu_half", "glu_ready", "sig_ready", "lin_ready", "mix_ready", "act_ready"))
    sgT_done, sgT_ready, aT_done, aT_ready = sem("sgT_done"), sem("sgT_ready"), sem("aT_done"), sem("aT_ready")
    y_ready, comb_done, comb_added = sem("y_ready"), sem("comb_done"), sem("comb_added")
    pp_done, pg_done, pg_sig, out_ready, out_done = (
        sem(n) for n in ("pp_done", "pg_done", "pg_sig", "out_ready", "out_done"))
    hsum, rstd_ready, ln_sq, ln_root = sem("hsum"), sem("rstd_ready"), sem("ln_sq"), sem("ln_root")
    pool_step = sem("pool_step")

    block = ctx.enter_context(nc.Block())

    G_V, G_UV, G_GA, G_GB = 6, 10, 16, 20
    UNITS = TB * SLOTS_PER_GROUP

    def unit(u):
        return u // TB, u % TB, u % TB + 1

    def early_read(k):
        if k < L_V:
            return proj_done, 2 * (k + 1)
        if k < L_UV:
            return proj_done, G_V + 2 * (k - L_V + 1)
        if k < L_GA:
            return proj_done, G_UV + 2 * (k - L_UV + 1)
        if k < L_ATT:
            return proj_done, G_GA + 2 * (k - L_GA + 1)
        if k < L_GB:
            return y_done, 4
        if k < L_GM:
            return proj_done, G_GB + 2 * (k - L_GB + 1)
        return (y_done, 8) if k < L_WO else (wo_done, TB)

    @block.sync
    def _(sp):
        xv = a["x"][0].rearrange("(b p) d -> p b d", p=P)
        sp.dma_start(h[:, :, :], xv).then_inc(x_in, 16)
        for k in range(n_early):
            if k >= EARLY:
                sp.wait_ge(*early_read(k - EARLY))
            sp.dma_start(early_slot(k), early_views[k]).then_inc(early_in[k % EARLY], 16)

        def moe_load(m, expert_pair):
            j, e = m // 2, 2 * expert_pair + m % 2
            src = w_up[bass.ds(e, 1), :, j * SLOT:(j + 1) * SLOT] if j < UPL else \
                w_dn[bass.ds(e, 1), :, (j - UPL) * SLOT:(j - UPL + 1) * SLOT]
            return src.rearrange("a p n -> p (a n)")

        for k in range(2 * LOADS):
            s = ORDER[k % RING]
            if k < RING:
                if s < EARLY:
                    last = max(n for n in range(n_early) if n % EARLY == s)
                    sp.wait_ge(*early_read(last))
                else:
                    sp.wait_ge(y_done, 8)
            else:
                sp.wait_ge(moe_free, k + 1)
            sp.dma_start(ring[:, s, :], moe_load(k % LOADS, k // LOADS)).then_inc(moe_in[s], 16)
        sp.wait_ge(count_ready, 1)
        n = sp.value_load(count[0:1, 0:1], min_val=PAIRS // 2, max_val=PASSES * PAIRS // 2)
        with sp.Fori(1, n) as i:
            for k in range(2 * LOADS):
                s = ORDER[k % RING]
                sp.wait_ge(moe_free, i * (2 * LOADS) + (k + 1))
                sp.dma_start(ring[:, s, :], moe_load(k % LOADS, 2 * (i % (PAIRS // 2)) + k // LOADS)).then_inc(
                    moe_in[s], 16)
        for k, (dst, src) in enumerate([(ring[:, ORDER[0], 0:2 * D].rearrange("p (c n) -> p c n", c=2), w_pp),
                                        (ring[:, ORDER[1], :], w_pg[:, 0:SLOT]),
                                        (ring[:, ORDER[2], :], w_pg[:, SLOT:2 * SLOT])]):
            sp.wait_ge(moe_free, n * (2 * LOADS) + (k + 1))
            sp.dma_start(dst, src).then_inc(ple_in[k], 16)
        ov = out[0].rearrange("(b p) d -> b p d", p=P)
        for b in range(TB):
            sp.wait_ge(out_ready, b + 1)
            sp.dma_start(ov[b], xn[:, b, :]).then_inc(out_done, 16)
        sp.wait_ge(out_done, 16 * TB)

    @block.gpsimd
    def _(pool):
        steps = [0]

        def link(ins):
            steps[0] += 1
            ins.then_inc(pool_step, 1)
            pool.wait_ge(pool_step, steps[0])

        def root(ready, got, var, src, dst, scale, done):
            pool.wait_ge(ready, got)
            link(pool.tensor_scalar(var, src, scale, EPS, ALU.mult, ALU.add))
            pool.tensor_tensor(dst, var, half, ALU.pow).then_inc(done, 1)

        def rms_root(k):
            root(sq_done, k + 1, rms_var[:, k:k + 1], mean_sq[:, k:k + 1], rstd[:, k:k + 1], 1.0, rstd_ready)

        link(pool.memset(half, -0.5))
        pool.dma_start(gain[:, :], a["g_moe"][0].partition_broadcast(P)).then_inc(gmoe_in, 16)
        pool.dma_start(wr[:, :, :], a["w_router"][0].rearrange("(p c) e -> p c e", c=KC)).then_inc(small_in, 16)
        pool.dma_start(brout, a["b_router"][0].partition_broadcast(P)).then_inc(small_in, 16)
        pool.dma_start(cols[:, 1, :], a["g_ple"][0].rearrange("(p c) -> p c", c=KC)).then_inc(small_in, 16)
        pool.dma_start(pick[:, :].bitcast(mybir.dt.uint16), a["pick_const"]).then_inc(small_in, 16)
        pool.dma_start(pT[:, :, :], a["p"]).then_inc(small_in, 16)
        pool.dma_start(bdown[:, :], a["b_down"][0]).then_inc(bdown_in, 16)
        for k in range(TB):
            rms_root(k)
        pool.wait_ge(xT_done, 1)
        pool.dma_start(lng, a["ln_v_g"][0].partition_broadcast(P)).then_inc(ln_in, 16)
        pool.dma_start(lnb, a["ln_v_b"][0].partition_broadcast(P)).then_inc(ln_in, 16)
        for b in range(TB):
            root(ln_sq, b + 1, ln_var[:, b:b + 1], ln_ss[:, b:b + 1], ln_rstd[:, b:b + 1], 1.0 / GM, ln_root)
        for k in range(2, 4):
            rms_root(k)
        pool.wait_ge(xn_ready, 4)
        pool.dma_start(gain[:, :], a["g_final"].partition_broadcast(P)).then_inc(gfin_in, 16)
        for k in range(4, 8):
            rms_root(k)

    @block.scalar
    def _(eng):
        steps = [0]

        def link(ins):
            steps[0] += 1
            ins.then_inc(act_step, 1)
            eng.wait_ge(act_step, steps[0])

        eng.dma_start(const[:, :], a["table_const"]).then_inc(const_in, 16)
        eng.dma_start(onehot, a["onehot_const"]).then_inc(rel_in, 16)
        eng.dma_start(relb[0:BUCKETS, :], a["rel_bias"]).then_inc(rel_in, 16)
        eng.dma_start(cols[:, 0, :], a["g_mix"][0].rearrange("(p c) -> p c", c=KC)).then_inc(const_in, 16)
        eng.dma_start(ws_raw, a["w_spatial"]).then_inc(ws_in, 16)
        eng.dma_start(bs[:, :], a["b_spatial"]).then_inc(ws_in, 16)
        for k in range(3):
            eng.dma_start(work[E * k:E * (k + 1), 0:2 * D], a["b_gate_up"][0]).then_inc(bgu_in, 16)

        def mean_square(k, src, junk):
            eng.activation(junk, src, ACT.Square, scale=D ** -0.5, accum_out=mean_sq[:, k:k + 1]).then_inc(sq_done, 1)

        eng.wait_ge(x_in, 16)
        for b in range(TB):
            mean_square(b, h[:, b, :], xn[:, b, :])
        eng.wait_ge(vals_ready, 1)
        for g in range(GROUPS):
            dst = skewed[g * SLOTS_PER_GROUP:(g + 1) * SLOTS_PER_GROUP, :, :]
            src = vals[:, g, :].unsqueeze(1).to_broadcast([SLOTS_PER_GROUP, P, SKEW])
            eng.dma_start(dst, src).then_inc(skew_out, 16)
        eng.wait_ge(skew_out, 16 * GROUPS)
        skew_read = bass.AP(skewed, P - 1, [[SKEW - 1, P], [P * SKEW, HEADS], [1, T]])
        eng.dma_start(btab, skew_read).then_inc(btab_in, 16)
        eng.wait_ge(const_in, 32)
        eng.wait_ge(xT_done, 1)
        for c in range(KC // 2):
            eng.activation(xt_all[:, c, :], bank(c // 2)[:, c % 2 * T:(c % 2 + 1) * T], ACT.Identity,
                           scale=cols[:, 0, c:c + 1]).then_inc(xT_ready, 1)

        def evac(g, dst, n, func=ACT.Copy):
            eng.wait_ge(proj_done, g + 1)
            eng.activation(dst, bank(g % 3)[:, 0:n], func).then_inc(proj_free, 1)

        for g in range(G_V):
            evac(g, qkT[:, 2 * g:2 * g + 2, :].rearrange("p c t -> p (c t)"), BLKN)
        for g in range(4):
            c0, n = (0, BLKN) if g < 2 else (BLKN, QKV - BLKN)
            evac(G_V + g, vsb[:, g % TB, c0:c0 + n], n)
        for u in range(UNITS):
            nk = unit(u)[2] * P
            eng.wait_ge(nm_ready, u + 1)
            eng.activation(prob[:, u % 2, :, 0:nk], prob[:, u % 2, :, 0:nk], ACT.Exp, bias=neg_max[:, u:u + 1],
                           accum_out=den[:, u:u + 1]).then_inc(exp_done, 1)
            if 1 <= u < 7:
                g = u - 1
                if g == 0:
                    eng.wait_ge(bgu_ready, 1)
                evac(G_UV + g, uv[:, g % TB, g // TB * BLKN:(g // TB + 1) * BLKN], BLKN)
            eng.wait_ge(pT_done, u + 1)
            if u:
                eng.wait_ge(pv_done, u)
            eng.activation(probT[:, 0:3 * nk], bank(5, 2)[:, 0:3 * nk], ACT.Copy).then_inc(pT_ready, 1)
        eng.wait_ge(proj_free, G_GA)
        for b in range(TB):
            eng.activation(uv[:, b, GM:], uv[:, b, GM:], ACT.Gelu, accum_out=ln_sum[:, b:b + 1]).then_inc(gelu_done, 1)
        for b in range(TB):
            eng.activation(uv[:, b, 0:GM], uv[:, b, 0:GM], ACT.Gelu).then_inc(gelu_done, 1)
        eng.wait_ge(pv_done, UNITS)
        eng.activation(attT.rearrange("p c t -> p (c t)"), bank(7), ACT.Copy).then_inc(att_ready, 1)
        for k in range(4):
            if k >= 2:
                eng.wait_ge(y_read, k - 1)
            evac(G_GA + k, sig[:, k % 2, :], BLKN, ACT.Sigmoid)
        for k in range(4):
            if k == 2:
                eng.wait_ge(gT_done, 1)
                eng.activation(gT.rearrange("p c t -> p (c t)"), bank(3, 3), ACT.Copy).then_inc(gT_ready, 1)
            eng.wait_ge(y_read, 4 + k - 1)
            evac(G_GB + k, sig[:, k % 2, :], BLKN, ACT.Sigmoid)
        for b in range(TB):
            eng.wait_ge(mT_done, b + 1)
            eng.activation(xt_tb[:, b, :, :].rearrange("p c t -> p (c t)"), bank(2 * b, 2), ACT.Copy).then_inc(
                mT_ready, 1)

        def norm_and_transpose(k0):
            for b in range(TB):
                eng.wait_ge(h_ready, b + 1)
                mean_square(k0 + b, h[:, b, :], xn[:, b, :])

        norm_and_transpose(2)
        for b in range(TB):
            eng.wait_ge(xT_done, 2 + b)
            eng.activation(xt_route[:, b, :, :].rearrange("p c t -> p (c t)"), bank(2 * b, 2), ACT.Copy).then_inc(
                xT_ready, 1)
        eng.wait_ge(top_sub, TB)
        eng.activation(top_e, top_e, ACT.Exp).then_inc(top_exp, 1)
        eng.wait_ge(gatesT_done, 1)
        eng.activation(gatesT.rearrange("p b t -> p (b t)"), bank(7)[0:E, 0:T], ACT.Copy).then_inc(gatesT_ready, 1)

        def gathered(pair, q):
            eng.wait_ge(xg_done, pair + 1)
            eng.activation(xt_tb[:, q, :, :].rearrange("p c t -> p (c t)"), bank(6, 2), ACT.Copy).then_inc(xg_ready, 1)

        gathered(0, 0)
        eng.wait_ge(count_ready, 1)
        n = eng.value_load(count[0:1, 0:1], min_val=PAIRS // 2, max_val=PASSES * PAIRS // 2)
        with eng.Fori(0, n) as i:
            for q in range(2):
                pair = 2 * i + q
                for s in range(2):
                    eng.wait_ge(glu_ready, pair * 2 + (s + 1))
                    eng.activation(sigm[:, s, :], glu[:, s, :], ACT.Sigmoid, scale=ALPHA).then_inc(sig_ready, 1)
                gathered(pair + 1, 1 - q)
                eng.wait_ge(sgT_done, pair + 1)
                eng.activation(selgT.rearrange("p b t -> p (b t)"), bank(2)[:, 0:T], ACT.Copy).then_inc(sgT_ready, 1)
                for s in range(2):
                    eng.wait_ge(aT_done, pair * 2 + (s + 1))
                    eng.activation(actT[:, 4 * s:4 * s + 4, :].rearrange("p c t -> p (c t)"), bank(s),
                                   ACT.Copy).then_inc(aT_ready, 1)
                eng.wait_ge(moe_free, pair * LOADS + (RING + LOADS))
                eng.activation(ysb, bank(4, 2), ACT.Copy).then_inc(y_ready, 1)
        for b in range(TB):
            eng.wait_ge(comb_added, n * 4 + 2)
            mean_square(4 + b, h[:, b, :], xn[:, b, :])
        for b in range(TB):
            eng.wait_ge(xT_done, 4 + b)
            for c in range(KC // 2):
                eng.activation(xt_tb[:, b, c, :], bank(2 * b + c // 4)[:, (c % 4) * P:(c % 4 + 1) * P], ACT.Identity,
                               scale=cols[:, 1, c:c + 1]).then_inc(xT_ready, 1)
        for b in range(TB):
            eng.wait_ge(pg_done, b + 1)
            eng.activation(stage[:, b * D:(b + 1) * D], bank(2 * b, 2), ACT.Sigmoid).then_inc(pg_sig, 1)
        for b in range(TB):
            eng.wait_ge(hsum, b + 1)
            mean_square(6 + b, h[:, b, :], xn[:, b, :])

    @block.vector
    def _(eng):
        steps = [0]

        def link(ins):
            steps[0] += 1
            ins.then_inc(dve_step, 1)
            eng.wait_ge(dve_step, steps[0])

        def normalise(k, dst, src, by=None):
            eng.wait_ge(rstd_ready, k + 1)
            if by is None:
                return eng.tensor_scalar(dst, src, rstd[:, k:k + 1], None, ALU.mult)
            return eng.scalar_tensor_tensor(out=dst, in0=src, scalar=rstd[:, k:k + 1], in1=by, op0=ALU.mult,
                                            op1=ALU.mult)

        link(eng.memset(relb[BUCKETS:BUCKETS + 1, :], 1.0))
        eng.memset(ones[:, :], 1.0).then_inc(ones_ready, 1)
        for b in range(TB):
            normalise(b, xn[:, b, :], h[:, b, :]).then_inc(xn_ready, 1)
        eng.wait_ge(vals_done, 1)
        eng.tensor_copy(vals, ps[0:SLOTS_PER_GROUP, 4:7, 0:SKEW]).then_inc(vals_ready, 1)
        eng.wait_ge(xT_done, 1)
        for c in range(KC // 2, KC):
            eng.tensor_scalar(xt_all[:, c, :], bank(c // 2)[:, c % 2 * T:(c % 2 + 1) * T], cols[:, 0, c:c + 1], None,
                              ALU.mult).then_inc(xT_ready2, 1)
        eng.wait_ge(ws_in, 32)
        eng.wait_ge(const_in, 32)
        eng.tensor_tensor(wsT, ws_raw,
                          tril_t.unsqueeze(1).to_broadcast([P, GMG, P]), ALU.mult).then_inc(ws_ready, 1)
        eng.wait_ge(bgu_in, 48)
        link(eng.tensor_copy(bias_gu[:, :], raw_bgu))
        for k in (1, 2):
            for r in range(k, 3):
                rows = slice(E * r, E * (r + 1))
                link(eng.tensor_tensor(work[rows, 0:2 * D], work[rows, 0:2 * D], bias_gu[rows, :], ALU.subtract))
                last = eng.tensor_copy(bias_gu[rows, :], work[rows, 0:2 * D])
                if (k, r) != (2, 2):
                    link(last)
        last.then_inc(bgu_ready, 1)

        eng.wait_ge(btab_in, 16)
        for u in range(UNITS):
            s, b, kb = unit(u)
            nk, off, w = kb * P, (TB - kb) * P, prob[:, u % 2, :, 0:kb * P]
            eng.wait_ge(qk_done, u + 1)
            if u >= 2:
                eng.wait_ge(pT_done, u - 1)
            eng.scalar_tensor_tensor(out=w, in0=bank(3, 2)[:, 0:3 * T].rearrange("p (g s) -> p g s", g=GROUPS)[
                :, :, 0:nk], scalar=HD ** -0.5, in1=btab[:, s::SLOTS_PER_GROUP, off:off + nk], op0=ALU.mult,
                op1=ALU.add).then_inc(qk_read, 1)
            eng.wait_ge(qk_read, u + 1)
            link(eng.tensor_reduce(row_max[:, u:u + 1], w, AX.XY, ALU.max))
            eng.tensor_scalar(neg_max[:, u:u + 1], row_max[:, u:u + 1], -1.0, None, ALU.mult).then_inc(nm_ready, 1)
            eng.wait_ge(exp_done, u + 1)
            link(eng.reciprocal(rden[:, u:u + 1], den[:, u:u + 1]))
            eng.tensor_scalar(w, w, rden[:, u:u + 1], None, ALU.mult).then_inc(prob_ready, 1)
        eng.wait_ge(ln_in, 32)
        eng.wait_ge(pT_done, UNITS)
        for b in range(TB):
            v = uv[:, b, GM:]
            eng.wait_ge(gelu_done, b + 1)
            link(eng.tensor_scalar(ln_nm[:, b:b + 1], ln_sum[:, b:b + 1], -1.0 / GM, None, ALU.mult))
            link(eng.tensor_scalar(v, v, ln_nm[:, b:b + 1], None, ALU.add))
            eng.tensor_tensor_reduce(stage[:, 0:GM], v, v, 1.0, 0.0, ALU.mult, ALU.add,
                                     ln_ss[:, b:b + 1]).then_inc(ln_sq, 1)
            eng.wait_ge(ln_root, b + 1)
            link(eng.scalar_tensor_tensor(out=v, in0=v, scalar=ln_rstd[:, b:b + 1], in1=lng, op0=ALU.mult,
                                          op1=ALU.mult))
            ins = eng.tensor_tensor(v, v, lnb, ALU.add)
            ins.then_inc(vn_ready, 1)
        eng.wait_ge(vn_ready, 2)
        for k in range(4):
            n, b = k // TB, k % TB
            eng.wait_ge(proj_free, G_GA + k + 1)
            eng.wait_ge(y_done, k + 1)
            eng.tensor_tensor(xn[:, b, n * BLKN:(n + 1) * BLKN], bank(3 + k % 2), sig[:, k % 2, :],
                              ALU.mult).then_inc(y_read, 1)
        eng.wait_ge(mixed_done, 1)
        eng.wait_ge(ws_in, 32)
        eng.wait_ge(gelu_done, 4)
        for b in range(TB):
            v = uv[:, b, GM:].rearrange("p (g d) -> p g d", g=GMG)
            mixed = bank(3, 3).rearrange("p (g b d) -> p g b d", g=GMG, b=TB)[:, :, b, :]
            eng.tensor_tensor(v, mixed, bs[:, :].unsqueeze(2).to_broadcast([P, GMG, HD]), ALU.add).then_inc(
                mixed_read, 1)
            eng.wait_ge(mixed_read, b + 1)
            eng.tensor_tensor(uv[:, b, GM:], uv[:, b, GM:], uv[:, b, 0:GM], ALU.mult).then_inc(g_ready, 1)
        for k in range(4):
            n, b = k // TB, k % TB
            m = xn[:, b, n * BLKN:(n + 1) * BLKN]
            eng.wait_ge(proj_free, G_GB + k + 1)
            eng.wait_ge(y_done, 4 + k + 1)
            if k == 0:
                eng.wait_ge(y_read, 4)
            eng.tensor_tensor(gated, bank(6 + k % 2), sig[:, k % 2, :], ALU.mult).then_inc(y_read, 1)
            eng.wait_ge(y_read, 4 + k + 1)
            eng.tensor_tensor(m, m, gated, ALU.add).then_inc(merged_ready, 1)
            eng.wait_ge(merged_ready, k + 1)
        for b in range(TB):
            eng.wait_ge(wo_done, b + 1)
            eng.tensor_tensor(h[:, b, :], h[:, b, :], bank(4 + 2 * b, 2), ALU.add).then_inc(h_ready, 1)
            if b == 0:
                eng.wait_ge(gmoe_in, 16)
            eng.wait_ge(h_ready, b + 1)
            normalise(2 + b, xn[:, b, :], h[:, b, :], gain[:, :]).then_inc(xn_ready, 1)

        eng.wait_ge(small_in, 80)
        for b in range(TB):
            eng.wait_ge(rt_done, b + 1)
            link(eng.tensor_tensor(logits[:, b, :], bank(4 + b)[:, 0:E], brout, ALU.add))
            link(eng.max(top_v[:, b, :], logits[:, b, :]))
            link(eng.max_index(top_i[:, b, :], top_v[:, b, :], logits[:, b, :]))
        for b in range(TB):
            ins = eng.tensor_scalar(top_e[:, b, :], top_v[:, b, 0:TOP], top_v[:, b, 0:1], None, ALU.subtract)
            ins.then_inc(top_sub, 1)
        for b in range(TB):
            link(eng.tensor_tensor(chosen[:, b, :, :], iota[:, 0:E].unsqueeze(1).to_broadcast([P, TOP, E]),
                                   top_i[:, b, 0:TOP].unsqueeze(2).to_broadcast([P, TOP, E]), ALU.is_equal))
        eng.tensor_reduce(mask, chosen.rearrange("p b k e -> p b e k"), AX.X, ALU.add).then_inc(mask_ready, 1)
        eng.wait_ge(top_exp, 1)
        link(eng.tensor_reduce(top_s, top_e, AX.X, ALU.add))
        link(eng.reciprocal(top_r, top_s))
        link(eng.tensor_tensor(top_g, top_e, top_r.unsqueeze(2).to_broadcast([P, TB, TOP]), ALU.mult))
        for b in range(TB):
            link(eng.tensor_tensor(weighted[:, b, :, :], chosen[:, b, :, :],
                                   top_g[:, b, :].unsqueeze(2).to_broadcast([P, TOP, E]), ALU.mult))
        eng.tensor_reduce(gates, weighted.rearrange("p b k e -> p b e k"), AX.X, ALU.add).then_inc(gates_ready, 1)
        eng.wait_ge(rank_done, 1)
        eng.wait_ge(mask_ready, 1)
        ranks = bank(6)[:, 0:2 * E].rearrange("p (b e) -> p b e", b=TB)
        link(eng.scalar_tensor_tensor(out=rank1, in0=ranks, scalar=1.0, in1=mask, op0=ALU.add, op1=ALU.mult))
        eng.memset(rank_of[:, :, PASSES * E:], -1.0).then_inc(dve_step, 1)
        eng.memset(gate_of[:, :, PASSES * E:], 0.0).then_inc(dve_step, 1)
        steps[0] += 2
        for r in range(PASSES):
            steps[0] += 1
            eng.tensor_scalar(rank_of[:, :, r * E:(r + 1) * E], rank1, -1.0 - CAP * r, None, ALU.add).then_inc(
                dve_step, 1)
        eng.wait_ge(gates_ready, 1)
        for r in range(PASSES):
            steps[0] += 1
            eng.tensor_copy(gate_of[:, :, r * E:(r + 1) * E], gates).then_inc(dve_step, 1)
        eng.wait_ge(dve_step, steps[0])

        def select(pair, q):
            r2 = rank_of[:, :, bass.ds(pair * 2, 2)].unsqueeze(3).to_broadcast([P, TB, 2, CAP])
            g2 = gate_of[:, :, bass.ds(pair * 2, 2)].unsqueeze(3).to_broadcast([P, TB, 2, CAP])
            io = iota.unsqueeze(1).unsqueeze(1).to_broadcast([P, TB, 2, CAP])
            s4 = sel[:, q, :, :].rearrange("p b (e s) -> p b e s", e=2)
            g4 = selg[:, q, :, :].rearrange("p b (e s) -> p b e s", e=2)
            eng.tensor_tensor(s4, io, r2, ALU.is_equal).then_inc(sel_ready, 1)
            eng.wait_ge(sel_ready, pair * 2 + 1)
            eng.tensor_tensor(g4, s4, g2, ALU.mult).then_inc(sel_ready, 1)

        select(0, 0)
        totals = bank(6)[:, 2 * E:3 * E]
        link(eng.tensor_reduce(fullest, totals, AX.X, ALU.max))
        for r in range(1, PASSES):
            link(eng.tensor_scalar(passes[:, r:r + 1], fullest, float(CAP * r), PAIRS / 2, ALU.is_gt, ALU.mult))
        link(eng.tensor_reduce(passes[:, 0:1], passes[:, 1:PASSES], AX.X, ALU.add))
        eng.tensor_scalar(count[:, :], passes[:, 0:1], PAIRS / 2, None, ALU.add).then_inc(count_ready, 1)
        for b in (1, 0):
            eng.wait_ge(bd_done, TB - b)
            eng.tensor_tensor(h[:, b, :], h[:, b, :], bank(2 if b else 4, 2), ALU.add).then_inc(comb_added, 1)

        eng.wait_ge(count_ready, 1)
        n = eng.value_load(count[0:1, 0:1], min_val=PAIRS // 2, max_val=PASSES * PAIRS // 2)
        with eng.Fori(0, n) as i:
            for q in range(2):
                pair = 2 * i + q
                select(pair + 1, 1 - q)
                for s in range(2):
                    k = pair * 2 + (s + 1)
                    if s == 0:
                        eng.wait_ge(gu_half, pair + 1)
                    else:
                        eng.wait_ge(moe_free, pair * LOADS + (RING + 2 * UPL))
                    eng.tensor_scalar(glu[:, s, :], bank(s), LIMIT, None, ALU.min).then_inc(glu_ready, 1)
                    eng.tensor_scalar(lin[:, s, :], bank(2 + s), LIMIT, -LIMIT, ALU.min, ALU.max).then_inc(
                        lin_ready, 1)
                    eng.wait_ge(glu_ready, k)
                    eng.wait_ge(lin_ready, k)
                    eng.scalar_tensor_tensor(out=lin[:, s, :], in0=lin[:, s, :], scalar=1.0, in1=glu[:, s, :],
                                             op0=ALU.add, op1=ALU.mult).then_inc(mix_ready, 1)
                    eng.wait_ge(mix_ready, k)
                    eng.wait_ge(sig_ready, k)
                    eng.tensor_tensor(act[:, s * BLKN:(s + 1) * BLKN], lin[:, s, :], sigm[:, s, :],
                                      ALU.mult).then_inc(act_ready, 1)
                for b in (1, 0):
                    eng.wait_ge(comb_done, pair * 2 + (2 - b))
                    eng.wait_ge(comb_added, pair * 2 + (3 - b))
                    eng.tensor_tensor(h[:, b, :], h[:, b, :], bank(2 if b else 6, 2), ALU.add).then_inc(
                        comb_added, 1)
        eng.wait_ge(comb_added, n * 4 + 2)
        for b in range(TB):
            normalise(4 + b, xn[:, b, :], h[:, b, :]).then_inc(xn_ready, 1)
        for b in range(TB):
            eng.wait_ge(xT_done, 4 + b)
            for c in range(KC // 2, KC):
                eng.tensor_scalar(xt_tb[:, b, c, :], bank(2 * b + c // 4)[:, (c % 4) * P:(c % 4 + 1) * P],
                                  cols[:, 1, c:c + 1], None, ALU.mult).then_inc(xT_ready2, 1)
        eng.wait_ge(pp_done, 1)
        eng.wait_ge(gfin_in, 16)
        for b in range(TB):
            eng.wait_ge(pg_sig, b + 1)
            link(eng.tensor_tensor(stage[:, b * D:(b + 1) * D], stage[:, b * D:(b + 1) * D], bank(4 + 2 * b, 2),
                                   ALU.mult))
            eng.tensor_tensor(h[:, b, :], h[:, b, :], stage[:, b * D:(b + 1) * D], ALU.add).then_inc(hsum, 1)
        for b in range(TB):
            normalise(6 + b, xn[:, b, :], h[:, b, :], gain[:, :]).then_inc(out_ready, 1)

    @block.tensor
    def _(eng):
        def early(k):
            eng.wait_ge(early_in[k % EARLY], 16 * (k // EARLY + 1))
            return early_slot(k)

        eng.wait_ge(rel_in, 32)
        eng.wait_ge(ones_ready, 1)
        for g in range(GROUPS):
            last = eng.matmul(bank(4 + g)[0:SLOTS_PER_GROUP, 0:SKEW],
                              relb[:, g * SLOTS_PER_GROUP:(g + 1) * SLOTS_PER_GROUP], onehot[:, g, :], start=True,
                              stop=True)
        last.then_inc(vals_done, 1)
        eng.wait_ge(const_in, 32)
        for b in range(TB):
            eng.wait_ge(xn_ready, b + 1)
            for c in range(KC):
                last = eng.transpose(bank(c // 2)[:, c % 2 * T + b * P:c % 2 * T + (b + 1) * P], xn[:, b, c::KC], ident)
        last.then_inc(xT_done, 1)

        def group(g):
            if g >= 3:
                eng.wait_ge(proj_free, g - 2)
            else:
                eng.wait_ge(xT_ready, KC // 2)
                eng.wait_ge(xT_ready2, KC // 2)
            return bank(g % 3)

        for g in range(G_V):
            w, o = early(L_QK + g // 2), group(g)
            for f in range(2):
                c0 = (g % 2 * 2 + f) * P
                for c in range(KC):
                    last = eng.matmul(o[:, f * T:(f + 1) * T], w[:, c, c0:c0 + P], xt_all[:, c, :], start=c == 0,
                                      stop=c == KC - 1)
            last.then_inc(proj_done, 1)

        def rows(g, load, c0=0, n=BLKN, b=0):
            w, o = early(load), group(g)
            for c in range(KC):
                last = eng.matmul(o[:, 0:n], xt_all[:, c, b * P:(b + 1) * P], w[:, c, c0:c0 + n], start=c == 0,
                                  stop=c == KC - 1)
            last.then_inc(proj_done, 1)

        def unit_logits(u):
            s, b, kb = unit(u)
            eng.wait_ge(proj_free, G_V)
            if u:
                eng.wait_ge(qk_read, u)
            for g in range(GROUPS):
                hd = g * SLOTS_PER_GROUP + s
                r = slice(HD * (hd % 2), HD * (hd % 2 + 1))
                last = eng.matmul(bank(3, 2)[:, g * T:g * T + kb * P], qkT[r, hd // 2, b * P:(b + 1) * P],
                                  qkT[r, 6 + hd // 2, 0:kb * P], start=True, stop=True)
            last.then_inc(qk_done, 1)

        def unit_transpose(u):
            s, b, kb = unit(u)
            eng.wait_ge(prob_ready, u + 1)
            if u:
                eng.wait_ge(pT_ready, u)
            for g in range(GROUPS):
                for k in range(kb):
                    o = (g * kb + k) * P
                    last = eng.transpose(bank(5, 2)[:, o:o + P], prob[:, u % 2, g, k * P:(k + 1) * P], ident)
            last.then_inc(pT_done, 1)

        def unit_values(u):
            s, b, kb = unit(u)
            eng.wait_ge(pT_ready, u + 1)
            eng.wait_ge(proj_free, G_UV)
            o = bank(7)[HD * (s % 2):HD * (s % 2 + 1), s // 2 * T + b * P:s // 2 * T + (b + 1) * P]
            for g in range(GROUPS):
                for k in range(kb):
                    hd, t = g * SLOTS_PER_GROUP + s, (g * kb + k) * P
                    last = eng.matmul(o, vsb[:, k, hd * HD:(hd + 1) * HD], probT[:, t:t + P],
                                      start=g == 0 and k == 0, stop=g == GROUPS - 1 and k == kb - 1)
            last.then_inc(pv_done, 1)

        unit_logits(0)
        for g in range(4):
            rows(G_V + g, L_V + g // 2, 0, BLKN if g < 2 else QKV - BLKN, g % TB)
        unit_transpose(0)
        for u in range(1, UNITS):
            unit_logits(u)
            if u < 7:
                rows(G_UV + u - 1, L_UV + (u - 1) // TB, b=(u - 1) % TB)
            else:
                rows(G_GA, L_GA, b=0)
            unit_values(u - 1)
            unit_transpose(u)
        unit_values(UNITS - 1)

        def attention_out(k):
            n, b = k // TB, k % TB
            w = early(L_ATT)
            eng.wait_ge(att_ready, 1)
            if k >= 2:
                eng.wait_ge(y_read, k - 1)
            for c in range(2):
                last = eng.matmul(bank(3 + k % 2), attT[:, c, b * P:(b + 1) * P], w[:, c, n * BLKN:(n + 1) * BLKN],
                                  start=c == 0, stop=c == 1)
            last.then_inc(y_done, 1)

        def gmlp_out(k):
            n, b = k // TB, k % TB
            eng.wait_ge(gT_ready, 1)
            if k >= 2:
                eng.wait_ge(y_read, 4 + k - 1)
            for c in range(6):
                w = early(L_GM + c // 3)
                last = eng.matmul(bank(6 + k % 2), gT[:, c, b * P:(b + 1) * P],
                                  w[:, c % 3, n * BLKN:(n + 1) * BLKN], start=c == 0, stop=c == 5)
            last.then_inc(y_done, 1)

        for k in range(4):
            if k:
                rows(G_GA + k, L_GA + k // TB, b=k % TB)
            if k % 2:
                attention_out(k - 1)
                attention_out(k)
        eng.wait_ge(ws_ready, 1)
        eng.wait_ge(vn_ready, TB)
        eng.wait_ge(y_read, 4)
        for g in range(GMG):
            last = eng.matmul(bank(3, 3)[:, g * P:(g + 1) * P], wsT[:, g, :],
                              uv[:, :, GM + g * HD:GM + (g + 1) * HD], start=True, stop=True)
        last.then_inc(mixed_done, 1)
        rows(G_GB, L_GB, b=0)
        rows(G_GB + 1, L_GB, b=1)
        for b in range(TB):
            eng.wait_ge(g_ready, b + 1)
            eng.wait_ge(mixed_read, TB)
            for c in range(6):
                last = eng.transpose(bank(3, 3)[:, c * T + b * P:c * T + (b + 1) * P],
                                     uv[:, b, GM + c * P:GM + (c + 1) * P], ident)
        last.then_inc(gT_done, 1)
        rows(G_GB + 2, L_GB + 1, b=0)
        gmlp_out(0)
        gmlp_out(1)
        rows(G_GB + 3, L_GB + 1, b=1)
        gmlp_out(2)
        gmlp_out(3)

        for b in range(TB):
            eng.wait_ge(merged_ready, 3 + b)
            eng.wait_ge(proj_free, G_GB + 4)
            for c in range(KC):
                last = eng.transpose(bank(2 * b, 2)[:, c * P:(c + 1) * P], xn[:, b, c::KC], ident)
            last.then_inc(mT_done, 1)
        for b in range(TB):
            eng.wait_ge(mT_ready, b + 1)
            if b:
                eng.wait_ge(y_read, 8)
            for c in range(KC):
                w = early(L_WO + c // 4)
                for n in range(NB):
                    last = eng.matmul(bank(4 + 2 * b + n), xt_tb[:, b, c, :], w[:, c % 4, n * BLKN:(n + 1) * BLKN],
                                      start=c == 0, stop=c == KC - 1)
            last.then_inc(wo_done, 1)

        eng.wait_ge(small_in, 80)
        for b in range(TB):
            eng.wait_ge(xn_ready, 3 + b)
            for c in range(KC):
                last = eng.transpose(bank(2 * b, 2)[:, c * P:(c + 1) * P], xn[:, b, c::KC], ident)
            last.then_inc(xT_done, 1)
        for b in range(TB):
            eng.wait_ge(xT_ready, KC // 2 + b + 1)
            for c in range(KC):
                last = eng.matmul(bank(4 + b)[:, 0:E], xt_route[:, b, c, :], wr[:, c, :], start=c == 0,
                                  stop=c == KC - 1)
            last.then_inc(rt_done, 1)
        eng.wait_ge(mask_ready, 1)
        eng.matmul(bank(6)[:, 0:E], before, mask[:, 0, :], start=True, stop=True).then_inc(moe_free, RING)
        eng.matmul(bank(6)[:, E:2 * E], ones[:, :], mask[:, 0, :], start=True, stop=False)
        eng.matmul(bank(6)[:, E:2 * E], before, mask[:, 1, :], start=False, stop=True)
        eng.matmul(bank(6)[:, 2 * E:3 * E], ones[:, :], mask[:, 0, :], start=True, stop=False)
        eng.matmul(bank(6)[:, 2 * E:3 * E], ones[:, :], mask[:, 1, :], start=False, stop=True).then_inc(rank_done, 1)
        eng.wait_ge(gates_ready, 1)
        for b in range(TB):
            last = eng.transpose(bank(7)[0:E, b * P:(b + 1) * P], gates[:, b, :], ident)
        last.then_inc(gatesT_done, 1)
        eng.wait_ge(gatesT_ready, 1)
        eng.wait_ge(bdown_in, 16)
        for b in (1, 0):
            for n in range(NB):
                last = eng.matmul(bank((2 if b else 4) + n), gatesT[:, b, :], bdown[:, n * BLKN:(n + 1) * BLKN],
                                  start=True, stop=True)
            last.then_inc(bd_done, 1)

        def gather(pair, q):
            eng.wait_ge(sel_ready, pair * 2 + 1)
            for c in range(KC):
                for b in range(TB):
                    last = eng.matmul(bank(6, 2)[:, c * P:(c + 1) * P], xn[:, b, c::KC], sel[:, q, b, :],
                                      start=b == 0, stop=b == TB - 1)
            last.then_inc(xg_done, 1)

        eng.wait_ge(count_ready, 1)
        gather(0, 0)
        n = eng.value_load(count[0:1, 0:1], min_val=PAIRS // 2, max_val=PASSES * PAIRS // 2)
        with eng.Fori(0, n) as i:
            for q in range(2):
                pair = 2 * i + q

                def arrived(m):
                    k = q * LOADS + m
                    s = ORDER[k % RING]
                    eng.wait_ge(moe_in[s], i * (16 * 2 * LOADS // RING) + 16 * (k // RING + 1))
                    return ring[:, s, :].rearrange("p (c n) -> p c n", n=2 * D if m < 2 * UPL else D)

                def both(o, x, w, cw, n0, stop):
                    for e in range(2):
                        r = slice(CAP * e, CAP * (e + 1))
                        last = eng.matmul(o[r, :], x[:, r], w[e][:, cw, n0:n0 + BLKN], start=False, stop=stop,
                                          skip_group_check=True)
                        yield last

                eng.wait_ge(comb_added, pair * 2 + 1)
                eng.wait_ge(xg_ready, pair + 1)
                for k in range(4):
                    eng.matmul(bank(k), pick[:, bass.ds((i % (PAIRS // 2)) * (2 * P) + q * P, P)],
                               bias_gu[:, k * BLKN:(k + 1) * BLKN], start=True, stop=False, skip_group_check=True)
                for j in range(UPL):
                    w = [arrived(2 * j + e) for e in range(2)]
                    order = [(c, k) for c in range(2) for k in range(4)] if j < UPL - 1 else \
                        [(c, k) for half in range(2) for c in range(2) for k in (half, half + 2)]
                    for at, (c, k) in enumerate(order):
                        ends = j == UPL - 1 and c == 1
                        even, odd = both(bank(k), xt_tb[:, q, 2 * j + c, :], w, c, k * BLKN, ends)
                        if at == 7:
                            even.then_inc(moe_free, 1)
                            odd.then_inc(moe_free, 1)
                        elif ends and at == 3:
                            odd.then_inc(gu_half, 1)
                eng.wait_ge(comb_added, pair * 2 + 2)
                gather(pair + 1, 1 - q)
                eng.wait_ge(act_ready, pair * 2 + 2)
                for b in range(TB):
                    last = eng.transpose(bank(2)[:, b * P:(b + 1) * P], selg[:, q, b, :], ident)
                last.then_inc(sgT_done, 1)
                for s in range(2):
                    for c in range(4):
                        last = eng.transpose(bank(s)[:, c * P:(c + 1) * P], act[:, 4 * s + c::KC], ident)
                    last.then_inc(aT_done, 1)
                for j in range(2):
                    w = [arrived(2 * (UPL + j) + e) for e in range(2)]
                    eng.wait_ge(aT_ready, pair * 2 + (j + 1))
                    for c in range(4):
                        for k in range(NB):
                            first = j == 0 and c == 0
                            for e in range(2):
                                r = slice(CAP * e, CAP * (e + 1))
                                last = eng.matmul(bank(4 + k)[r, :], actT[:, 4 * j + c, r],
                                                  w[e][:, c, k * BLKN:(k + 1) * BLKN], start=first,
                                                  stop=j == 1 and c == 3, skip_group_check=True)
                                if c == 3 and k == NB - 1:
                                    last.then_inc(moe_free, 1)
                eng.wait_ge(sgT_ready, pair + 1)
                eng.wait_ge(y_ready, pair + 1)
                eng.wait_ge(xg_ready, pair + 2)
                for b in (1, 0):
                    for k in range(NB):
                        last = eng.matmul(bank((2 if b else 6) + k), selgT[:, b, :], ysb[:, k * BLKN:(k + 1) * BLKN],
                                          start=True, stop=True)
                    last.then_inc(comb_done, 1)

        eng.wait_ge(ple_in[0], 16)
        wpp = ring[:, ORDER[0], 0:2 * D].rearrange("p (c n) -> p c n", c=2)
        for b in range(TB):
            if b:
                eng.wait_ge(comb_added, n * 4 + 2)
            for k in range(NB):
                for c in range(2):
                    last = eng.matmul(bank(4 + 2 * b + k), pT[:, c, b * P:(b + 1) * P],
                                      wpp[:, c, k * BLKN:(k + 1) * BLKN], start=c == 0, stop=c == 1)
        last.then_inc(pp_done, 1)
        for b in range(TB):
            eng.wait_ge(xn_ready, 5 + b)
            for c in range(KC):
                last = eng.transpose(bank(2 * b, 2)[:, c * P:(c + 1) * P], xn[:, b, c::KC], ident)
            last.then_inc(xT_done, 1)
        for k in (1, 2):
            eng.wait_ge(ple_in[k], 16)
        wpg = [ring[:, ORDER[1 + k], :].rearrange("p (c n) -> p c n", n=D) for k in range(2)]
        for b in range(TB):
            eng.wait_ge(xT_ready, KC // 2 * (b + 2) + TB)
            eng.wait_ge(xT_ready2, KC // 2 * (b + 2))
            for c in range(KC):
                for k in range(NB):
                    last = eng.matmul(bank(2 * b + k), xt_tb[:, b, c, :], wpg[c // 4][:, c % 4, k * BLKN:(k + 1) * BLKN],
                                      start=c == 0, stop=c == KC - 1)
            last.then_inc(pg_done, 1)


def constants():
    import numpy as np

    table = np.zeros((P, CONSTS), np.float32)
    table[:, IDENT:IDENT + P] = np.eye(P)
    table[:, TRIL:TRIL + P] = np.triu(np.ones((P, P)))
    table[:, BEFORE:BEFORE + P] = np.triu(np.ones((P, P)), 1)
    table[:, IOTA:IOTA + CAP] = np.arange(CAP)
    onehot = np.zeros((BUCKETS + 1, GROUPS, SKEW), np.float32)
    exact = BUCKETS // 2
    for g, (window, dilation) in enumerate(((128, 1), (512, 4), (2048, 16))):
        for u in range(SKEW):
            dist = T - 1 - u
            if dist < 0 or dist > window or dist % dilation:
                onehot[BUCKETS, g, u] = -(2.0 ** 100)
                continue
            nf = np.maximum(np.int64(dist), 1).astype(np.float32)
            large = exact + (np.log(nf / exact) / np.log(2048 / exact) * (BUCKETS - exact)).astype(np.int32)
            onehot[dist if dist < exact else min(int(large), BUCKETS - 1), g, u] = 1.0
    pick = np.zeros((3, E, PAIRS, 2, CAP), np.float32)
    for e in range(E):
        pick[:, e, e // 2, e % 2, :] = 1.0
    return {"table_const": table, "onehot_const": onehot,
            "pick_const": pick.reshape(3 * E, PAIRS * P).astype(np.uint16) * np.uint16(BF16_ONE)}


_INS = ["x", "p", "g_mix", "w_in", "rel_bias", "w_att_out", "ln_v_g", "ln_v_b", "w_spatial", "b_spatial",
        "w_gmlp_out", "w_out", "g_moe", "w_router", "b_router", "w_gate_up", "b_gate_up", "w_down", "b_down",
        "g_ple", "w_ple_gate", "w_ple_proj", "g_final"]


def kernel(**inputs):
    import numpy as _np
    import concourse.bacc as _bacc
    from concourse import mybir as _mybir
    from concourse.bass_utils import run_bass_kernel_spmd as _run

    w_in = _np.asarray(inputs["w_in"])[0].reshape(P, KC, -1)
    cuts = _np.cumsum(in_widths())[:-1]
    inputs = dict(inputs, w_in=_np.concatenate([w.reshape(P, -1) for w in _np.split(w_in, cuts, axis=2)], axis=1),
                  p=_np.asarray(inputs["p"])[0, 0].T.reshape(P, 2, T),
                  w_spatial=_np.asarray(inputs["w_spatial"])[0].transpose(2, 0, 1),
                  b_spatial=_np.asarray(inputs["b_spatial"])[0].T)
    nc = _bacc.Bacc("TRN2", target_bir_lowering=False, num_devices=1)
    arrays, aps = {}, {}
    for name, a in list({k: inputs[k] for k in _INS}.items()) + list(constants().items()):
        a = _np.ascontiguousarray(a)
        arrays[f"in_{name}"] = a
        aps[name] = nc.dram_tensor(f"in_{name}", a.shape, _mybir.dt.from_np(a.dtype), kind="ExternalInput").ap()
    out = nc.dram_tensor("out_0", (1, T, D), _mybir.dt.float32, kind="ExternalOutput").ap()
    with ExitStack() as ctx:
        build(nc, ctx, aps, out)
    r = _run(nc, [arrays], core_ids=[0])
    return r.results[0]["out_0"]
```

```python
from contextlib import ExitStack

import concourse.bass as bass
import concourse.mybir as mybir

F32 = mybir.dt.float32
F32R = mybir.dt.float32r
BF16 = mybir.dt.bfloat16
I32 = mybir.dt.int32
U32 = mybir.dt.uint32
ALU = mybir.AluOpType
ACT = mybir.ActivationFunctionType
AX = mybir.AxisListType

P = 128
D = 1024
KC = D // P
TB = 2
T = TB * P
HD = 64
SLOTS_PER_GROUP = 4
GROUPS = 3
HEADS = GROUPS * SLOTS_PER_GROUP
QKV = HEADS * HD
GM = 768
GMG = 12
UV0 = 3 * QKV
GATE0 = UV0 + 2 * GM
BLKN = 512
NB = D // BLKN
E = 32
TOP = 4
CAP = 64
PAIRS = E // 2
PASSES = T // CAP
BUCKETS = 32
SKEW = 384
EPS = 1e-6
BF16_ONE = 0x3F80
LIMIT = 7.0
ALPHA = 1.702
SLOT = 4096
RING = 8
RAW = 3
SCRATCH = 6
ORDER = [5, 6, 7, 3, 4, 0, 1, 2]
PIECE = 2048
LOADS = 12
UPL = 4
IDENT, TRIL, BEFORE, IOTA, CONSTS = 0, 128, 256, 384, 448


def in_widths():
    return [BLKN] * 4 + [QKV - BLKN] + [BLKN] * 7


def build(nc, ctx, a, out):
    def sb(name, shape, dt=F32):
        return ctx.enter_context(nc.sbuf_tensor(name, shape, dt))

    def sem(name):
        return ctx.enter_context(nc.semaphore(name))

    with ExitStack() as until_moe:
        def split(name, shape):
            return until_moe.enter_context(nc.sbuf_tensor(name, shape, F32R))

        w_hi, w_lo = split("w_hi", [P, 2, PIECE]), split("w_lo", [P, 2, PIECE])
        x_hi, x_lo = split("x_hi", [P, 2 * D]), split("x_lo", [P, 2 * D])
        until_moe.enter_context(nc.sbuf_tensor("loads", [P, RAW, SLOT], F32))
        g_hi, g_lo = split("g_hi", [P, 6, T]), split("g_lo", [P, 6, T])
        a_hi, a_lo = split("a_hi", [P, 2, T]), split("a_lo", [P, 2, T])
    ring = sb("ring", [P, RING, SLOT])
    h = sb("h", [P, TB, D])
    xn = sb("xn", [P, TB, D])
    xt = sb("xt", [P, 2 * D])
    stage = sb("stage", [P, 3 * D])
    work = sb("work", [P, 3 * D])
    late = sb("late", [P, 1536])
    bias = sb("bias", [3 * E, 3 * D], BF16)
    pick = sb("pick", [3 * E, PAIRS * P], BF16)
    pT = sb("pT", [P, 2, T])
    gain = sb("gain", [P, D])
    const = sb("const", [P, CONSTS])
    wr = sb("wr", [P, KC, E])
    rank_of = sb("rank_of", [P, TB, PASSES * E + 4])
    gate_of = sb("gate_of", [P, TB, PASSES * E + 4])
    cols = sb("cols", [P, 3, KC])
    bs = sb("bs", [P, GMG])
    ones = sb("ones", [P, P])
    tiny = sb("tiny", [P, 96])
    route = sb("route", [P, 96])
    count = sb("count", [P, 1], I32)
    top_i = sb("top_i", [P, TB, 8], U32)
    ps = ctx.enter_context(nc.psum_tensor("ps", [P, 8, BLKN], F32))

    ident = const[:, IDENT:IDENT + P]
    before = const[:, BEFORE:BEFORE + P]
    tril_t = const[:, TRIL:TRIL + P]
    iota = const[:, IOTA:IOTA + CAP]
    xh_all, xl_all = (v[:, :].rearrange("p (c t) -> p c t", c=KC) for v in (x_hi, x_lo))
    xh_tb, xl_tb = (v[:, :].rearrange("p (b c t) -> p b c t", b=TB, c=KC) for v in (x_hi, x_lo))
    xt_tb = xt[:, :].rearrange("p (b c t) -> p b c t", b=TB, c=KC)
    scratch = ring[:, SCRATCH:RING, :].rearrange("p s n -> p (s n)")
    btab = scratch[:, 0:HEADS * T].rearrange("p (h s) -> p h s", h=HEADS)
    qkT = scratch[:, 3072:6144].rearrange("p (c t) -> p c t", c=12)
    vsb = scratch[:, 6144:7680].rearrange("p (b n) -> p b n", b=TB)
    prob = stage[:, 0:1536].rearrange("p (b g s) -> p b g s", b=2, g=GROUPS)
    probT = stage[:, 1536:2304]
    sig = xt[:, :].rearrange("p (b n) -> p b n", b=4)
    gated = stage[:, 2048:2560]
    ws_raw = stage[:, 0:1536].rearrange("p (g j) -> p g j", g=GMG)
    vals = stage[0:SLOTS_PER_GROUP, 1536:1536 + GROUPS * SKEW].rearrange("p (g u) -> p g u", g=GROUPS)
    xt_route = stage[:, 0:2048].rearrange("p (b c t) -> p b c t", b=TB, c=KC)
    uv = work[:, :].rearrange("p (b n) -> p b n", b=TB)
    onehot = late[0:BUCKETS + 1, 0:GROUPS * SKEW].rearrange("p (g u) -> p g u", g=GROUPS)
    wsT = late[:, :].rearrange("p (g i) -> p g i", g=GMG)
    lng, lnb = xn[:, 0, 0:GM], xn[:, 1, 0:GM]
    relb = tiny[0:BUCKETS + 1, 80:92]
    act = stage[:, 0:D]
    actT = stage[:, D:2 * D].rearrange("p (c t) -> p c t", c=KC)
    ysb = stage[:, 2 * D:3 * D]
    glu = work[:, 0:D].rearrange("p (b n) -> p b n", b=2)
    sigm = work[:, D:2 * D].rearrange("p (b n) -> p b n", b=2)
    lin = work[:, 2 * D:3 * D].rearrange("p (b n) -> p b n", b=2)
    sel = late[:, 0:512].rearrange("p (q b s) -> p q b s", q=2, b=TB)
    selg = late[:, 512:1024].rearrange("p (q b s) -> p q b s", q=2, b=TB)
    selgT = late[:, 1024:1280].rearrange("p (b t) -> p b t", b=TB)
    mean_sq, rstd = tiny[:, 0:8], tiny[:, 8:16]
    row_max, neg_max, den, rden = tiny[:, 16:24], tiny[:, 24:32], tiny[:, 32:40], tiny[:, 40:48]
    ln_sum, ln_nm, ln_ss, ln_var, ln_rstd = (tiny[:, 48 + 2 * k:50 + 2 * k] for k in range(5))
    rms_var = tiny[:, 64:72]
    half = tiny[:, 72:73]
    fullest, passes = tiny[:, 58:59], tiny[:, 59:63]
    top_v = route[:, 0:16].rearrange("p (b k) -> p b k", b=TB)
    top_e = route[:, 16:24].rearrange("p (b k) -> p b k", b=TB)
    top_s, top_r = route[:, 24:26], route[:, 26:28]
    top_g = route[:, 32:40].rearrange("p (b k) -> p b k", b=TB)
    brout = route[:, 40:72]
    logits = work[:, 0:64].rearrange("p (b e) -> p b e", b=TB)
    chosen = work[:, 64:320].rearrange("p (b k e) -> p b k e", b=TB, k=TOP)
    weighted = work[:, 320:576].rearrange("p (b k e) -> p b k e", b=TB, k=TOP)
    mask = work[:, 576:640].rearrange("p (b e) -> p b e", b=TB)
    gates = work[:, 640:704].rearrange("p (b e) -> p b e", b=TB)
    rank1 = work[:, 704:768].rearrange("p (b e) -> p b e", b=TB)

    def gate_ple(b, k):
        return stage[:, b * D + k * BLKN:b * D + (k + 1) * BLKN]

    skewed = nc.dram_tensor("skewed", [HEADS, P, SKEW], F32)

    def bank(k, n=1):
        return ps[:, k:k + n, :].rearrange("p b n -> p (b n)")

    w_out = a["w_out"][0].rearrange("(p c) n -> p c n", c=KC)
    w_gm = a["w_gmlp_out"][0].rearrange("(c p) n -> p c n", p=P)
    widths = in_widths()

    def w_in(k):
        c0 = sum(widths[:k])
        return a["w_in"][:, KC * c0:KC * (c0 + widths[k])].rearrange("p (c n) -> p c n", c=KC)

    early_views = [w_in(k) for k in range(10)]
    early_views += [a["w_att_out"][0].rearrange("(c p) n -> p c n", p=P)]
    early_views += [w_in(10), w_in(11)]
    early_views += [w_gm[:, 0:4, :], w_gm[:, 4:6, :], w_out[:, 0:4, :], w_out[:, 4:8, :]]
    (L_QK, L_V, L_UV, L_GA, L_ATT, L_GB, L_GM, L_WO) = (0, 3, 5, 8, 10, 11, 13, 15)
    n_early = len(early_views)

    def words(k):
        return early_views[k].shape[1] * early_views[k].shape[2]

    def halves(p, w):
        k, at = pieces[p]
        if k >= L_V:
            return early_slot(k)[:, at:at + PIECE], w[:, p % 2, :]
        n = PIECE // KC
        return (early_slot(k).rearrange("p (c n) -> p c n", c=KC)[:, :, at // KC:at // KC + n],
                w[:, p % 2, :].rearrange("p (c n) -> p c n", c=KC))

    def early_slot(k):
        return ring[:, RAW + k % RAW, 0:words(k)]

    pieces = [(k, w) for k in range(n_early) for w in range(0, words(k), PIECE)]
    first_piece = [min(i for i, (j, _) in enumerate(pieces) if j == k) for k in range(n_early)] + [len(pieces)]
    W_V, W_UV, W_GA, W_ATT, W_GB, W_GM, W_WO = (first_piece[k] for k in (L_V, L_UV, L_GA, L_ATT, L_GB, L_GM, L_WO))

    w_up = a["w_gate_up"][0].rearrange("e (p c) n -> e p (c n)", c=KC)
    w_dn = a["w_down"][0].rearrange("e (p c) n -> e p (c n)", c=KC)
    w_pp = a["w_ple_proj"][0].rearrange("(p c) n -> p c n", c=2)
    w_pg = a["w_ple_gate"][0].rearrange("(p c) n -> p (c n)", c=KC)

    x_in = [sem(f"x_in{b}") for b in range(TB)]
    const_in, bias_in, ws_in, small_in, ln_in, gmoe_in, gfin_in, rel_in, skew_out, btab_in = (
        sem(n) for n in ("const_in", "bias_in", "ws_in", "small_in", "ln_in", "gmoe_in", "gfin_in", "rel_in",
                         "skew_out", "btab_in"))
    first_in = sem("first_in")
    early_in = [sem(f"early_in{k}") for k in range(RAW)]
    hi_ready, lo_ready, piece_done = sem("hi_ready"), sem("lo_ready"), sem("piece_done")
    moe_in = [sem(f"moe_in{k}") for k in range(RING)]
    moe_free = sem("moe_free")
    ple_in = [sem(f"ple_in{k}") for k in range(3)]
    dve_step, act_step = sem("dve_step"), sem("act_step")
    ones_ready, bias_part, bias_rest, merged_ready = sem("ones_ready"), sem("bias_part"), sem("bias_rest"), sem("merged_ready")
    vals_done, vals_ready = sem("vals_done"), sem("vals_ready")
    sq_done, xn_ready, xT_done, xT_ready = sem("sq_done"), sem("xn_ready"), sem("xT_done"), sem("xT_ready")
    x_bank_done = sem("x_bank_done")
    xT_ready2 = sem("xT_ready2")
    ws_ready, wr_ready = sem("ws_ready"), sem("wr_ready")
    proj_done, proj_free = sem("proj_done"), sem("proj_free")
    qk_done, qk_read, nm_ready, exp_done, prob_ready = (
        sem(n) for n in ("qk_done", "qk_read", "nm_ready", "exp_done", "prob_ready"))
    pT_done, pT_ready, pv_done, att_hi = sem("pT_done"), sem("pT_ready"), sem("pv_done"), sem("att_hi")
    att_ready, gT_hi, mT_hi = sem("att_ready"), sem("gT_hi"), sem("mT_hi")
    gelu_done, vn_ready, mixed_done, mixed_read, g_ready, gT_done, gT_ready = (
        sem(n) for n in ("gelu_done", "vn_ready", "mixed_done", "mixed_read", "g_ready", "gT_done", "gT_ready"))
    y_done, y_read = sem("y_done"), sem("y_read")
    mT_done, mT_ready, wo_done, h_ready = sem("mT_done"), sem("mT_ready"), sem("wo_done"), sem("h_ready")
    rt_done, mask_ready, top_sub, top_exp, rank_done, count_ready = (
        sem(n) for n in ("rt_done", "mask_ready", "top_sub", "top_exp", "rank_done", "count_ready"))
    sel_ready, xg_done, xg_ready = sem("sel_ready"), sem("xg_done"), sem("xg_ready")
    gu_half, glu_ready, sig_ready, lin_ready, mix_ready, act_ready = (
        sem(n) for n in ("gu_half", "glu_ready", "sig_ready", "lin_ready", "mix_ready", "act_ready"))
    sgT_done, sgT_ready, aT_done, aT_ready = sem("sgT_done"), sem("sgT_ready"), sem("aT_done"), sem("aT_ready")
    y_ready, comb_done, comb_added = sem("y_ready"), sem("comb_done"), sem("comb_added")
    pp_done, pg_done, pg_sig, out_ready, out_done = (
        sem(n) for n in ("pp_done", "pg_done", "pg_sig", "out_ready", "out_done"))
    hsum, rstd_ready, ln_sq, ln_root = sem("hsum"), sem("rstd_ready"), sem("ln_sq"), sem("ln_root")
    pool_step = sem("pool_step")

    block = ctx.enter_context(nc.Block())

    G_V, G_UV, G_GA, G_GB = 6, 10, 16, 20
    UNITS = TB * SLOTS_PER_GROUP

    def unit(u):
        return u // TB, u % TB, u % TB + 1

    def group_piece(g):
        if g < G_V:
            return g
        k = (g // 2) if g < G_GB else g // 2 + 1
        return first_piece[k + 1] - 1

    @block.sync
    def _(sp):
        xv = a["x"][0].rearrange("(b p) d -> p b d", p=P)
        for b in range(TB):
            sp.dma_start(h[:, b, :], xv[:, b, :]).then_inc(x_in[b], 16)
        for k in range(n_early):
            if k >= RAW:
                sp.wait_ge(lo_ready, first_piece[k - RAW + 1])
            dst, src = early_slot(k).rearrange("p (c n) -> p c n", c=early_views[k].shape[1]), early_views[k]
            if k == 0:
                n = PIECE // KC
                sp.dma_start(dst[:, :, 0:n], src[:, :, 0:n]).then_inc(first_in, 16)
                dst, src = dst[:, :, n:], src[:, :, n:]
            sp.dma_start(dst, src).then_inc(early_in[k % RAW], 16)
            if k == 3:
                sp.wait_ge(vals_ready, 1)
                for g in range(GROUPS):
                    sp.dma_start(skewed[g * SLOTS_PER_GROUP:(g + 1) * SLOTS_PER_GROUP, :, :],
                                 vals[:, g, :].unsqueeze(1).to_broadcast([SLOTS_PER_GROUP, P, SKEW])).then_inc(
                        skew_out, 16)
            if k == 4:
                sp.wait_ge(skew_out, 16 * GROUPS)
                sp.dma_start(btab, bass.AP(skewed, P - 1, [[SKEW - 1, P], [P * SKEW, HEADS], [1, T]])).then_inc(
                    btab_in, 16)

        def moe_load(m, expert_pair):
            j, e = m // 2, 2 * expert_pair + m % 2
            src = w_up[bass.ds(e, 1), :, j * SLOT:(j + 1) * SLOT] if j < UPL else \
                w_dn[bass.ds(e, 1), :, (j - UPL) * SLOT:(j - UPL + 1) * SLOT]
            return src.rearrange("a p n -> p (a n)")

        for k in range(2 * LOADS):
            s = ORDER[k % RING]
            if k < RING:
                if RAW <= s < SCRATCH:
                    last = max(n for n in range(n_early) if n % RAW == s - RAW)
                    sp.wait_ge(lo_ready, first_piece[last + 1])
                elif s >= SCRATCH:
                    sp.wait_ge(piece_done, W_WO)
                else:
                    sp.wait_ge(piece_done, len(pieces))
            else:
                sp.wait_ge(moe_free, k + 1)
            sp.dma_start(ring[:, s, :], moe_load(k % LOADS, k // LOADS)).then_inc(moe_in[s], 16)
        sp.wait_ge(count_ready, 1)
        n = sp.value_load(count[0:1, 0:1], min_val=PAIRS // 2, max_val=PASSES * PAIRS // 2)
        with sp.Fori(1, n) as i:
            for k in range(2 * LOADS):
                s = ORDER[k % RING]
                sp.wait_ge(moe_free, i * (2 * LOADS) + (k + 1))
                sp.dma_start(ring[:, s, :], moe_load(k % LOADS, 2 * (i % (PAIRS // 2)) + k // LOADS)).then_inc(
                    moe_in[s], 16)
        for k, (dst, src) in enumerate([(ring[:, ORDER[0], 0:2 * D].rearrange("p (c n) -> p c n", c=2), w_pp),
                                        (ring[:, ORDER[1], :], w_pg[:, 0:SLOT]),
                                        (ring[:, ORDER[2], :], w_pg[:, SLOT:2 * SLOT])]):
            sp.wait_ge(moe_free, n * (2 * LOADS) + (k + 1))
            sp.dma_start(dst, src).then_inc(ple_in[k], 16)
        ov = out[0].rearrange("(b p) d -> b p d", p=P)
        for t, b in enumerate((1, 0)):
            sp.wait_ge(out_ready, t + 1)
            sp.dma_start(ov[b], xn[:, b, :]).then_inc(out_done, 16)
        sp.wait_ge(out_done, 16 * TB)

    @block.gpsimd
    def _(pool):
        steps = [0]

        def link(ins):
            steps[0] += 1
            ins.then_inc(pool_step, 1)
            pool.wait_ge(pool_step, steps[0])

        def root(ready, got, var, src, dst, scale, done):
            pool.wait_ge(ready, got)
            link(pool.tensor_scalar(var, src, scale, EPS, ALU.mult, ALU.add))
            pool.tensor_tensor(dst, var, half, ALU.pow).then_inc(done, 1)

        def rms_root(k):
            root(sq_done, k + 1, rms_var[:, k:k + 1], mean_sq[:, k:k + 1], rstd[:, k:k + 1], 1.0, rstd_ready)

        link(pool.memset(half, -0.5))
        for k in range(TB):
            rms_root(k)
        pool.wait_ge(piece_done, 1)
        pool.dma_start(gain[:, :], a["g_moe"][0].partition_broadcast(P)).then_inc(gmoe_in, 16)
        pool.dma_start(wr[:, :, :], a["w_router"][0].rearrange("(p c) e -> p c e", c=KC)).then_inc(small_in, 16)
        pool.dma_start(brout, a["b_router"][0].partition_broadcast(P)).then_inc(small_in, 16)
        pool.dma_start(cols[:, 1, :], a["g_ple"][0].rearrange("(p c) -> p c", c=KC)).then_inc(small_in, 16)
        pool.dma_start(cols[:, 2, :], a["g_moe"][0].rearrange("(p c) -> p c", c=KC)).then_inc(small_in, 16)
        pool.dma_start(pick[:, :].bitcast(mybir.dt.uint16), a["pick_const"]).then_inc(small_in, 16)
        pool.dma_start(pT[:, :, :], a["p"]).then_inc(small_in, 16)
        pool.wait_ge(x_bank_done, KC // 2)
        pool.dma_start(lng, a["ln_v_g"][0].partition_broadcast(P)).then_inc(ln_in, 16)
        pool.dma_start(lnb, a["ln_v_b"][0].partition_broadcast(P)).then_inc(ln_in, 16)
        for k, rows in enumerate((slice(0, 2 * E), slice(0, E))):
            pool.wait_ge(bias_part, k + 1)
            pool.tensor_tensor(work[rows, :], work[rows, :], bias[rows, :], ALU.subtract).then_inc(bias_rest, 1)
        pool.wait_ge(small_in, 96)
        pool.tensor_tensor(wr[:, :, :], wr[:, :, :], cols[:, 2, :].unsqueeze(2).to_broadcast([P, KC, E]),
                           ALU.mult).then_inc(wr_ready, 1)
        for b in range(TB):
            root(ln_sq, b + 1, ln_var[:, b:b + 1], ln_ss[:, b:b + 1], ln_rstd[:, b:b + 1], 1.0 / GM, ln_root)
        for k in range(2, 4):
            rms_root(k)
        pool.wait_ge(xn_ready, 4)
        pool.dma_start(gain[:, :], a["g_final"].partition_broadcast(P)).then_inc(gfin_in, 16)
        for k in range(4, 8):
            rms_root(k)

    @block.scalar
    def _(eng):
        steps = [0]

        def link(ins):
            steps[0] += 1
            ins.then_inc(act_step, 1)
            eng.wait_ge(act_step, steps[0])

        eng.dma_start(const[:, :], a["table_const"]).then_inc(const_in, 16)
        eng.dma_start(cols[:, 0, :], a["g_mix"][0].rearrange("(p c) -> p c", c=KC)).then_inc(const_in, 16)
        eng.dma_start(onehot, a["onehot_const"]).then_inc(rel_in, 16)
        eng.dma_start(relb[0:BUCKETS, :], a["rel_bias"]).then_inc(rel_in, 16)

        def mean_square(k, src, junk):
            eng.activation(junk, src, ACT.Square, scale=D ** -0.5, accum_out=mean_sq[:, k:k + 1]).then_inc(sq_done, 1)

        for b in range(TB):
            eng.wait_ge(x_in[b], 16)
            mean_square(b, h[:, b, :], xn[:, b, :])
        def high(p):
            k, w = pieces[p]
            if p == 0:
                eng.wait_ge(first_in, 16)
            elif w == 0 or p == 1:
                eng.wait_ge(early_in[k % RAW], 16 * (k // RAW + 1))
            if p >= 2:
                eng.wait_ge(piece_done, p - 1)
            raw, hi = halves(p, w_hi)
            eng.activation(hi, raw, ACT.Copy).then_inc(hi_ready, 1)

        def evac(g, dst, n, func=ACT.Copy):
            if g >= G_V and g % 2 == 0:
                eng.wait_ge(proj_done, (g - G_V) // 2 + 1)
            else:
                eng.wait_ge(piece_done, group_piece(g) + 1)
            eng.activation(dst, bank(g % 3)[:, 0:n], func).then_inc(proj_free, 1)

        high(0)
        eng.wait_ge(const_in, 32)
        for c in range(KC):
            eng.wait_ge(x_bank_done, c // 2 + 1)
            eng.activation(xh_all[:, c, :], bank(c // 2)[:, c % 2 * T:(c % 2 + 1) * T], ACT.Identity,
                           scale=cols[:, 0, c:c + 1]).then_inc(xT_ready, 1)
        high(1)
        for k in range(3):
            eng.dma_start(work[E * k:E * (k + 1), 0:2 * D], a["b_gate_up"][0]).then_inc(bias_in, 16)
            eng.dma_start(work[E * k:E * (k + 1), 2 * D:], a["b_down"][0]).then_inc(bias_in, 16)
        eng.dma_start(ws_raw, a["w_spatial"]).then_inc(ws_in, 16)
        eng.dma_start(bs[:, :], a["b_spatial"]).then_inc(ws_in, 16)

        def bias_high(k):
            if k:
                eng.wait_ge(bias_rest, k)
            else:
                eng.wait_ge(bias_in, 96)
            rows = slice(0, (3 - k) * E)
            eng.activation(bias[rows, :], work[rows, :], ACT.Copy).then_inc(bias_part, 1)

        for g in range(G_V):
            evac(g, qkT[:, 2 * g:2 * g + 2, :].rearrange("p c t -> p (c t)"), BLKN)
            high(g + 2)
            if g in (2, 4):
                bias_high(g // 2 - 1)

        def exponentials(u):
            nk = unit(u)[2] * P
            eng.wait_ge(nm_ready, u + 1)
            eng.activation(prob[:, u % 2, :, 0:nk], prob[:, u % 2, :, 0:nk], ACT.Exp, bias=neg_max[:, u:u + 1],
                           accum_out=den[:, u:u + 1]).then_inc(exp_done, 1)

        def weights_out(u):
            nk = unit(u)[2] * P
            eng.wait_ge(pT_done, u + 1)
            if u:
                eng.wait_ge(pv_done, u)
            else:
                eng.wait_ge(skew_out, 16 * GROUPS)
            eng.activation(probT[:, 0:3 * nk], bank(5, 2)[:, 0:3 * nk], ACT.Copy).then_inc(pT_ready, 1)

        high(W_V + 2)
        exponentials(0)
        bias_high(2)
        evac(G_V, vsb[:, 0, 0:BLKN], BLKN)
        evac(G_V + 1, vsb[:, 1, 0:BLKN], BLKN)
        high(W_UV)
        for b in range(TB):
            evac(G_V + 2 + b, vsb[:, b, BLKN:], QKV - BLKN)
        weights_out(0)
        for u in range(1, UNITS):
            high(W_UV + u)
            exponentials(u)
            if u in (2, 4, 6):
                if u == 2:
                    eng.wait_ge(bias_part, 3)
                for b in range(TB):
                    c0 = (u // 2 - 1) * BLKN
                    evac(G_UV + u - 2 + b, uv[:, b, c0:c0 + BLKN], BLKN)
            weights_out(u)
        high(W_GA + 2)
        evac(G_GA, sig[:, 0, :], BLKN, ACT.Sigmoid)
        evac(G_GA + 1, sig[:, 1, :], BLKN, ACT.Sigmoid)
        high(W_GA + 3)
        eng.wait_ge(proj_free, G_GA)
        for b in range(TB):
            eng.activation(uv[:, b, GM:], uv[:, b, GM:], ACT.Gelu, accum_out=ln_sum[:, b:b + 1]).then_inc(gelu_done, 1)
        eng.wait_ge(pv_done, UNITS)
        eng.activation(a_hi[:, :, :].rearrange("p c t -> p (c t)"), bank(7), ACT.Copy).then_inc(att_hi, 1)
        for b in range(TB):
            eng.activation(uv[:, b, 0:GM], uv[:, b, 0:GM], ACT.Gelu).then_inc(gelu_done, 1)
        high(W_ATT)
        evac(G_GA + 2, sig[:, 2, :], BLKN, ACT.Sigmoid)
        evac(G_GA + 3, sig[:, 3, :], BLKN, ACT.Sigmoid)
        for p in range(3):
            high(W_GB + p)
        for k in range(2):
            eng.wait_ge(y_read, k + 1)
            evac(G_GB + k, sig[:, k, :], BLKN, ACT.Sigmoid)
        high(W_GB + 3)
        high(W_GM)
        eng.wait_ge(gT_done, 1)
        for k in range(3):
            eng.activation(g_hi[:, 2 * k:2 * k + 2, :].rearrange("p c t -> p (c t)"), bank(3 + k), ACT.Copy).then_inc(
                gT_hi, 1)
        for k in (2, 3):
            eng.wait_ge(y_read, k + 1)
            evac(G_GB + k, sig[:, k, :], BLKN, ACT.Sigmoid)
        high(W_GM + 1)
        high(W_GM + 2)
        high(W_WO)
        for b in range(TB):
            eng.wait_ge(mT_done, b + 1)
            for k in range(2):
                eng.activation(xh_tb[:, b, 4 * k:4 * k + 4, :].rearrange("p c t -> p (c t)"), bank(2 * b + k),
                               ACT.Copy).then_inc(mT_hi, 1)
            if b == 0:
                high(W_WO + 1)
        high(W_WO + 2)
        high(W_WO + 3)

        for b in range(TB):
            if b == 0:
                eng.wait_ge(h_ready, 1)
                mean_square(2, h[:, 0, :], xn[:, 0, :])
            eng.wait_ge(xT_done, 1 + b)
            eng.activation(xt_route[:, b, :, :].rearrange("p c t -> p (c t)"), bank(2 * b, 2), ACT.Copy).then_inc(
                xT_ready, 1)
        eng.wait_ge(h_ready, 2)
        mean_square(3, h[:, 1, :], xn[:, 1, :])
        eng.wait_ge(top_sub, TB)
        eng.activation(top_e, top_e, ACT.Exp).then_inc(top_exp, 1)

        def gathered(pair, q):
            eng.wait_ge(xg_done, pair + 1)
            eng.activation(xt_tb[:, q, :, :].rearrange("p c t -> p (c t)"), bank(6, 2), ACT.Copy).then_inc(xg_ready, 1)

        gathered(0, 0)
        eng.wait_ge(count_ready, 1)
        n = eng.value_load(count[0:1, 0:1], min_val=PAIRS // 2, max_val=PASSES * PAIRS // 2)
        with eng.Fori(0, n) as i:
            for q in range(2):
                pair = 2 * i + q
                for s in range(2):
                    eng.wait_ge(glu_ready, pair * 2 + (s + 1))
                    eng.activation(sigm[:, s, :], glu[:, s, :], ACT.Sigmoid, scale=ALPHA).then_inc(sig_ready, 1)
                gathered(pair + 1, 1 - q)
                eng.wait_ge(sgT_done, pair + 1)
                eng.activation(selgT.rearrange("p b t -> p (b t)"), bank(2)[:, 0:T], ACT.Copy).then_inc(sgT_ready, 1)
                for s in range(2):
                    eng.wait_ge(aT_done, pair * 2 + (s + 1))
                    eng.activation(actT[:, 4 * s:4 * s + 4, :].rearrange("p c t -> p (c t)"), bank(s),
                                   ACT.Copy).then_inc(aT_ready, 1)
                eng.wait_ge(moe_free, pair * LOADS + (RING + LOADS))
                eng.activation(ysb, bank(4, 2), ACT.Copy).then_inc(y_ready, 1)
        for t, b in enumerate((1, 0)):
            eng.wait_ge(comb_added, n * 4 + (1 + t))
            mean_square(4 + t, h[:, b, :], xn[:, b, :])
        for t, b in enumerate((1, 0)):
            eng.wait_ge(xT_done, 3 + t)
            for c in range(KC // 2):
                eng.activation(xt_tb[:, b, c, :], bank(2 * b + c // 4)[:, (c % 4) * P:(c % 4 + 1) * P], ACT.Identity,
                               scale=cols[:, 1, c:c + 1]).then_inc(xT_ready, 1)
        for t, b in enumerate((1, 0)):
            for k in range(NB):
                eng.wait_ge(pg_done, NB * t + k + 1)
                eng.activation(gate_ple(b, k), bank(2 * b + k), ACT.Sigmoid).then_inc(pg_sig, 1)
            eng.wait_ge(hsum, NB * (t + 1))
            mean_square(6 + t, h[:, b, :], xn[:, b, :])

    @block.vector
    def _(eng):
        steps = [0]

        def link(ins):
            steps[0] += 1
            ins.then_inc(dve_step, 1)
            eng.wait_ge(dve_step, steps[0])

        def normalise(k, dst, src, by=None):
            eng.wait_ge(rstd_ready, k + 1)
            if by is None:
                return eng.tensor_scalar(dst, src, rstd[:, k:k + 1], None, ALU.mult)
            return eng.scalar_tensor_tensor(out=dst, in0=src, scalar=rstd[:, k:k + 1], in1=by, op0=ALU.mult,
                                            op1=ALU.mult)

        link(eng.memset(relb[BUCKETS:BUCKETS + 1, :], 1.0))
        eng.memset(ones[:, :], 1.0).then_inc(ones_ready, 1)
        for b in range(TB):
            normalise(b, xn[:, b, :], h[:, b, :]).then_inc(xn_ready, 1)
        def low(p):
            eng.wait_ge(hi_ready, p + 1)
            if p >= 2:
                eng.wait_ge(piece_done, p - 1)
            (raw, lo), (_, hi) = halves(p, w_lo), halves(p, w_hi)
            eng.tensor_tensor(lo, raw, hi.bitcast(F32), ALU.subtract).then_inc(lo_ready, 1)

        low(0)
        for c in range(KC):
            if c % 2 == 0:
                eng.wait_ge(xT_ready, c + 2)
            eng.scalar_tensor_tensor(out=xl_all[:, c, :], in0=bank(c // 2)[:, c % 2 * T:(c % 2 + 1) * T],
                                     scalar=cols[:, 0, c:c + 1], in1=xh_all[:, c, :].bitcast(F32), op0=ALU.mult,
                                     op1=ALU.subtract).then_inc(xT_ready2, 1)
        low(1)
        low(2)
        eng.wait_ge(vals_done, 1)
        eng.tensor_copy(vals, ps[0:SLOTS_PER_GROUP, 4:7, 0:SKEW]).then_inc(vals_ready, 1)
        for p in range(3, W_V):
            low(p)
        eng.wait_ge(ws_in, 32)
        eng.tensor_tensor(wsT, ws_raw, tril_t.unsqueeze(1).to_broadcast([P, GMG, P]), ALU.mult).then_inc(ws_ready, 1)
        low(W_V)

        def scores(u):
            s, b, kb = unit(u)
            nk, off, w = kb * P, (TB - kb) * P, prob[:, u % 2, :, 0:kb * P]
            eng.wait_ge(qk_done, u + 1)
            if u >= 2:
                eng.wait_ge(pT_done, u - 1)
            eng.scalar_tensor_tensor(out=w, in0=bank(3, 2)[:, 0:3 * T].rearrange("p (g s) -> p g s", g=GROUPS)[
                :, :, 0:nk], scalar=HD ** -0.5, in1=btab[:, s::SLOTS_PER_GROUP, off:off + nk], op0=ALU.mult,
                op1=ALU.add).then_inc(qk_read, 1)
            eng.wait_ge(qk_read, u + 1)
            link(eng.tensor_reduce(row_max[:, u:u + 1], w, AX.XY, ALU.max))
            eng.tensor_scalar(neg_max[:, u:u + 1], row_max[:, u:u + 1], -1.0, None, ALU.mult).then_inc(nm_ready, 1)

        def over_sum(u):
            w = prob[:, u % 2, :, 0:unit(u)[2] * P]
            eng.wait_ge(exp_done, u + 1)
            link(eng.reciprocal(rden[:, u:u + 1], den[:, u:u + 1]))
            eng.tensor_scalar(w, w, rden[:, u:u + 1], None, ALU.mult).then_inc(prob_ready, 1)

        low(W_V + 1)
        eng.wait_ge(btab_in, 16)
        eng.wait_ge(ws_ready, 1)
        scores(0)
        over_sum(0)
        low(W_V + 2)
        low(W_UV)
        for u in range(1, UNITS):
            scores(u)
            low(W_UV + u)
            over_sum(u)
        low(W_GA + 2)
        def centre(b):
            v = uv[:, b, GM:]
            eng.wait_ge(gelu_done, b + 1)
            link(eng.tensor_scalar(ln_nm[:, b:b + 1], ln_sum[:, b:b + 1], -1.0 / GM, None, ALU.mult))
            link(eng.tensor_scalar(v, v, ln_nm[:, b:b + 1], None, ALU.add))
            eng.tensor_tensor_reduce(stage[:, 0:GM], v, v, 1.0, 0.0, ALU.mult, ALU.add,
                                     ln_ss[:, b:b + 1]).then_inc(ln_sq, 1)

        def scale(b):
            v = uv[:, b, GM:]
            eng.wait_ge(ln_root, b + 1)
            link(eng.scalar_tensor_tensor(out=v, in0=v, scalar=ln_rstd[:, b:b + 1], in1=lng, op0=ALU.mult,
                                          op1=ALU.mult))
            eng.tensor_tensor(v, v, lnb, ALU.add).then_inc(vn_ready, 1)

        def attention_out(k):
            n, b = k // TB, k % TB
            eng.wait_ge(proj_free, G_GA + k + 1)
            y_wait(0, k, W_ATT + 1)
            eng.tensor_tensor(xn[:, b, n * BLKN:(n + 1) * BLKN], bank(3 + k), sig[:, k, :],
                              ALU.mult).then_inc(y_read, 1)

        def y_wait(before_these, k, pieces_then):
            if k < 3:
                eng.wait_ge(y_done, before_these + k + 1)
            else:
                eng.wait_ge(piece_done, pieces_then)

        eng.wait_ge(ln_in, 32)
        eng.wait_ge(pT_done, UNITS)
        low(W_GA + 3)
        centre(0)
        scale(0)
        eng.wait_ge(att_hi, 1)
        eng.tensor_tensor(a_lo[:, :, :].rearrange("p c t -> p (c t)"), bank(7),
                          a_hi[:, :, :].rearrange("p c t -> p (c t)").bitcast(F32), ALU.subtract).then_inc(att_ready, 1)
        low(W_ATT)
        centre(1)
        low(W_GB)
        scale(1)
        eng.wait_ge(vn_ready, TB)
        attention_out(0)
        attention_out(1)
        low(W_GB + 1)
        attention_out(2)
        attention_out(3)
        low(W_GB + 2)
        eng.wait_ge(mixed_done, 1)
        eng.wait_ge(gelu_done, 4)
        for b in range(TB):
            v = uv[:, b, GM:].rearrange("p (g d) -> p g d", g=GMG)
            mixed = bank(3, 3).rearrange("p (g b d) -> p g b d", g=GMG, b=TB)[:, :, b, :]
            eng.tensor_tensor(v, mixed, bs[:, :].unsqueeze(2).to_broadcast([P, GMG, HD]), ALU.add).then_inc(
                mixed_read, 1)
            eng.wait_ge(mixed_read, b + 1)
            eng.tensor_tensor(uv[:, b, GM:], uv[:, b, GM:], uv[:, b, 0:GM], ALU.mult).then_inc(g_ready, 1)
        low(W_GB + 3)
        low(W_GM)
        for k in range(3):
            eng.wait_ge(gT_hi, k + 1)
            eng.tensor_tensor(g_lo[:, 2 * k:2 * k + 2, :].rearrange("p c t -> p (c t)"), bank(3 + k),
                              g_hi[:, 2 * k:2 * k + 2, :].rearrange("p c t -> p (c t)").bitcast(F32),
                              ALU.subtract).then_inc(gT_ready, 1)
        low(W_GM + 1)
        low(W_GM + 2)

        def merge(k):
            b, n = k // NB, k % NB
            m = xn[:, b, n * BLKN:(n + 1) * BLKN]
            eng.wait_ge(proj_free, G_GB + 4)
            y_wait(3, k, W_WO)
            eng.tensor_tensor(gated, bank(4 + k), sig[:, TB * n + b, :], ALU.mult).then_inc(y_read, 1)
            eng.wait_ge(y_read, 4 + k + 1)
            eng.tensor_tensor(m, m, gated, ALU.add).then_inc(merged_ready, 1)
            eng.wait_ge(merged_ready, k + 1)

        def merged_low(b):
            for k in range(2):
                eng.wait_ge(mT_hi, 2 * b + k + 1)
                eng.tensor_tensor(xl_tb[:, b, 4 * k:4 * k + 4, :].rearrange("p c t -> p (c t)"), bank(2 * b + k),
                                  xh_tb[:, b, 4 * k:4 * k + 4, :].rearrange("p c t -> p (c t)").bitcast(F32),
                                  ALU.subtract).then_inc(mT_ready, 1)

        for b in range(TB):
            merge(NB * b)
            merge(NB * b + 1)
            if b == 0:
                low(W_WO)
            merged_low(b)
        low(W_WO + 1)
        low(W_WO + 2)
        low(W_WO + 3)
        for b in range(TB):
            eng.wait_ge(*((piece_done, len(pieces)) if b else (wo_done, 1)))
            eng.tensor_tensor(h[:, b, :], h[:, b, :], bank(4 + 2 * b, 2), ALU.add).then_inc(h_ready, 1)
        eng.wait_ge(gmoe_in, 16)

        eng.wait_ge(small_in, 96)
        for b in range(TB):
            eng.wait_ge(h_ready, b + 1)
            normalise(2 + b, xn[:, b, :], h[:, b, :], gain[:, :]).then_inc(xn_ready, 1)
            eng.wait_ge(rt_done, b + 1)
            link(eng.scalar_tensor_tensor(out=logits[:, b, :], in0=bank(4 + b)[:, 0:E], scalar=rstd[:, 2 + b:3 + b],
                                          in1=brout, op0=ALU.mult, op1=ALU.add))
            link(eng.max(top_v[:, b, :], logits[:, b, :]))
            link(eng.max_index(top_i[:, b, :], top_v[:, b, :], logits[:, b, :]))
            link(eng.tensor_tensor(chosen[:, b, :, :], iota[:, 0:E].unsqueeze(1).to_broadcast([P, TOP, E]),
                                   top_i[:, b, 0:TOP].unsqueeze(2).to_broadcast([P, TOP, E]), ALU.is_equal))
            link(eng.tensor_reduce(mask[:, b, :], chosen[:, b, :, :].rearrange("p k e -> p e k"), AX.X, ALU.add))
            if b == 1:
                eng.memset(rank_of[:, :, PASSES * E:], -1.0).then_inc(mask_ready, 1)
            eng.tensor_scalar(top_e[:, b, :], top_v[:, b, 0:TOP], top_v[:, b, 0:1], None, ALU.subtract).then_inc(
                top_sub, 1)
        eng.wait_ge(top_exp, 1)
        link(eng.tensor_reduce(top_s, top_e, AX.X, ALU.add))
        link(eng.reciprocal(top_r, top_s))
        link(eng.tensor_tensor(top_g, top_e, top_r.unsqueeze(2).to_broadcast([P, TB, TOP]), ALU.mult))
        for b in range(TB):
            link(eng.tensor_tensor(weighted[:, b, :, :], chosen[:, b, :, :],
                                   top_g[:, b, :].unsqueeze(2).to_broadcast([P, TOP, E]), ALU.mult))
        link(eng.tensor_reduce(gates, weighted.rearrange("p b k e -> p b e k"), AX.X, ALU.add))
        for r in range(PASSES):
            steps[0] += 1
            eng.tensor_copy(gate_of[:, :, r * E:(r + 1) * E], gates).then_inc(dve_step, 1)
        eng.memset(gate_of[:, :, PASSES * E:], 0.0).then_inc(comb_added, 2)
        eng.wait_ge(dve_step, steps[0])
        eng.wait_ge(comb_added, 2)
        eng.wait_ge(mask_ready, 1)
        eng.wait_ge(rank_done, 1)
        ranks = bank(3)[:, 0:2 * E].rearrange("p (b e) -> p b e", b=TB)
        link(eng.scalar_tensor_tensor(out=rank1, in0=ranks, scalar=1.0, in1=mask, op0=ALU.add, op1=ALU.mult))
        for r in range(PASSES):
            steps[0] += 1
            eng.tensor_scalar(rank_of[:, :, r * E:(r + 1) * E], rank1, -1.0 - CAP * r, None, ALU.add).then_inc(
                dve_step, 1)
        eng.wait_ge(dve_step, steps[0])

        def select(pair, q):
            r2 = rank_of[:, :, bass.ds(pair * 2, 2)].unsqueeze(3).to_broadcast([P, TB, 2, CAP])
            g2 = gate_of[:, :, bass.ds(pair * 2, 2)].unsqueeze(3).to_broadcast([P, TB, 2, CAP])
            io = iota.unsqueeze(1).unsqueeze(1).to_broadcast([P, TB, 2, CAP])
            s4 = sel[:, q, :, :].rearrange("p b (e s) -> p b e s", e=2)
            g4 = selg[:, q, :, :].rearrange("p b (e s) -> p b e s", e=2)
            eng.tensor_tensor(s4, io, r2, ALU.is_equal).then_inc(sel_ready, 1)
            eng.wait_ge(sel_ready, pair * 2 + 1)
            eng.tensor_tensor(g4, s4, g2, ALU.mult).then_inc(sel_ready, 1)

        select(0, 0)
        link(eng.tensor_reduce(fullest, bank(3)[:, 2 * E:3 * E], AX.X, ALU.max))
        for r in range(1, PASSES):
            link(eng.tensor_scalar(passes[:, r:r + 1], fullest, float(CAP * r), PAIRS / 2, ALU.is_gt, ALU.mult))
        link(eng.tensor_reduce(passes[:, 0:1], passes[:, 1:PASSES], AX.X, ALU.add))
        eng.tensor_scalar(count[:, :], passes[:, 0:1], PAIRS / 2, None, ALU.add).then_inc(count_ready, 1)
        eng.wait_ge(count_ready, 1)
        n = eng.value_load(count[0:1, 0:1], min_val=PAIRS // 2, max_val=PASSES * PAIRS // 2)
        with eng.Fori(0, n) as i:
            for q in range(2):
                pair = 2 * i + q
                select(pair + 1, 1 - q)
                for s in range(2):
                    k = pair * 2 + (s + 1)
                    if s == 0:
                        eng.wait_ge(gu_half, pair + 1)
                    else:
                        eng.wait_ge(moe_free, pair * LOADS + (RING + 2 * UPL))
                    eng.tensor_scalar(glu[:, s, :], bank(s), LIMIT, None, ALU.min).then_inc(glu_ready, 1)
                    eng.tensor_scalar(lin[:, s, :], bank(2 + s), LIMIT, -LIMIT, ALU.min, ALU.max).then_inc(
                        lin_ready, 1)
                    eng.wait_ge(glu_ready, k)
                    eng.wait_ge(lin_ready, k)
                    eng.scalar_tensor_tensor(out=lin[:, s, :], in0=lin[:, s, :], scalar=1.0, in1=glu[:, s, :],
                                             op0=ALU.add, op1=ALU.mult).then_inc(mix_ready, 1)
                    eng.wait_ge(mix_ready, k)
                    eng.wait_ge(sig_ready, k)
                    eng.tensor_tensor(act[:, s * BLKN:(s + 1) * BLKN], lin[:, s, :], sigm[:, s, :],
                                      ALU.mult).then_inc(act_ready, 1)
                for b in (1, 0):
                    eng.wait_ge(comb_done, pair * 2 + (2 - b))
                    eng.wait_ge(comb_added, pair * 2 + (3 - b))
                    eng.tensor_tensor(h[:, b, :], h[:, b, :], bank(2 if b else 6, 2), ALU.add).then_inc(
                        comb_added, 1)
        eng.wait_ge(comb_added, n * 4 + 2)
        for t, b in enumerate((1, 0)):
            normalise(4 + t, xn[:, b, :], h[:, b, :]).then_inc(xn_ready, 1)
        for t, b in enumerate((1, 0)):
            eng.wait_ge(xT_done, 3 + t)
            for c in range(KC // 2, KC):
                eng.tensor_scalar(xt_tb[:, b, c, :], bank(2 * b + c // 4)[:, (c % 4) * P:(c % 4 + 1) * P],
                                  cols[:, 1, c:c + 1], None, ALU.mult).then_inc(xT_ready2, 1)
        eng.wait_ge(pp_done, 1)
        eng.wait_ge(gfin_in, 16)
        for t, b in enumerate((1, 0)):
            for k in range(NB):
                part = h[:, b, k * BLKN:(k + 1) * BLKN]
                eng.wait_ge(pg_sig, NB * t + k + 1)
                link(eng.tensor_tensor(gate_ple(b, k), gate_ple(b, k), bank(4 + 2 * b + k), ALU.mult))
                eng.tensor_tensor(part, part, gate_ple(b, k), ALU.add).then_inc(hsum, 1)
            normalise(6 + t, xn[:, b, :], h[:, b, :], gain[:, :]).then_inc(out_ready, 1)

    @block.tensor
    def _(eng):
        def three(o, a, b, first, last):
            eng.matmul(o, a[0], b[0], start=first, stop=False)
            eng.matmul(o, a[1], b[0], start=False, stop=False)
            return eng.matmul(o, a[0], b[1], start=False, stop=last)

        def weights(p, n):
            eng.wait_ge(hi_ready, p + 1)
            eng.wait_ge(lo_ready, p + 1)
            return [v[:, p % 2, :].rearrange("p (c n) -> p c n", n=n) for v in (w_hi, w_lo)]

        eng.wait_ge(const_in, 32)
        for b in range(TB):
            eng.wait_ge(xn_ready, b + 1)
            for c in range(KC):
                last = eng.transpose(bank(c // 2)[:, c % 2 * T + b * P:c % 2 * T + (b + 1) * P], xn[:, b, c::KC], ident)
                if b == TB - 1 and c % 2:
                    last.then_inc(x_bank_done, 1)

        def group(g):
            if g >= 3:
                eng.wait_ge(proj_free, g - 2)
            elif g:
                eng.wait_ge(xT_ready2, 2 * g + 2)
            return bank(g % 3)

        def relative_bias():
            eng.wait_ge(rel_in, 32)
            eng.wait_ge(ones_ready, 1)
            for g in range(GROUPS):
                last = eng.matmul(bank(4 + g)[0:SLOTS_PER_GROUP, 0:SKEW],
                                  relb[:, g * SLOTS_PER_GROUP:(g + 1) * SLOTS_PER_GROUP], onehot[:, g, :], start=True,
                                  stop=True)
            last.then_inc(vals_done, 1)

        def features(p):
            w, o = weights(p, PIECE // KC), group(p)
            for f in range(2):
                for c in range(KC):
                    if p == 0 and f == 0:
                        eng.wait_ge(xT_ready, c + 1)
                        eng.wait_ge(xT_ready2, max(c + 1, 2))
                    last = three(o[:, f * T:(f + 1) * T], [v[:, c, f * P:(f + 1) * P] for v in w],
                                 (xh_all[:, c, :], xl_all[:, c, :]), c == 0, c == KC - 1)
            last.then_inc(piece_done, 1)

        def rows(p, g, n=BLKN):
            w, per = weights(p, n), PIECE // n
            c0 = 0 if per == KC else (p - first_piece[pieces[p][0]]) * per
            for b in range(TB):
                o = group(g + b)[:, 0:n]
                for c in range(per):
                    r = slice(b * P, (b + 1) * P)
                    last = three(o, (xh_all[:, c0 + c, r], xl_all[:, c0 + c, r]), [v[:, c, :] for v in w],
                                 c0 + c == 0, c0 + c == KC - 1)
                if b == 0 and c0 + per == KC:
                    last.then_inc(proj_done, 1)
            last.then_inc(piece_done, 1)

        def unit_logits(u):
            s, b, kb = unit(u)
            eng.wait_ge(proj_free, G_V)
            eng.wait_ge(vals_ready, 1)
            if u:
                eng.wait_ge(qk_read, u)
            for g in range(GROUPS):
                hd = g * SLOTS_PER_GROUP + s
                r = slice(HD * (hd % 2), HD * (hd % 2 + 1))
                last = eng.matmul(bank(3, 2)[:, g * T:g * T + kb * P], qkT[r, hd // 2, b * P:(b + 1) * P],
                                  qkT[r, 6 + hd // 2, 0:kb * P], start=True, stop=True)
            last.then_inc(qk_done, 1)

        def unit_transpose(u):
            s, b, kb = unit(u)
            eng.wait_ge(prob_ready, u + 1)
            if u:
                eng.wait_ge(pT_ready, u)
            for g in range(GROUPS):
                for k in range(kb):
                    o = (g * kb + k) * P
                    last = eng.transpose(bank(5, 2)[:, o:o + P], prob[:, u % 2, g, k * P:(k + 1) * P], ident)
            last.then_inc(pT_done, 1)

        def unit_values(u):
            s, b, kb = unit(u)
            eng.wait_ge(pT_ready, u + 1)
            eng.wait_ge(proj_free, G_UV)
            o = bank(7)[HD * (s % 2):HD * (s % 2 + 1), s // 2 * T + b * P:s // 2 * T + (b + 1) * P]
            for g in range(GROUPS):
                for k in range(kb):
                    hd, t = g * SLOTS_PER_GROUP + s, (g * kb + k) * P
                    last = eng.matmul(o, vsb[:, k, hd * HD:(hd + 1) * HD], probT[:, t:t + P],
                                      start=g == 0 and k == 0, stop=g == GROUPS - 1 and k == kb - 1)
            last.then_inc(pv_done, 1)

        for p in range(W_V):
            features(p)
            if p == 0:
                relative_bias()
        rows(W_V, G_V)
        unit_logits(0)
        rows(W_V + 1, G_V)
        rows(W_V + 2, G_V + 2, QKV - BLKN)
        unit_transpose(0)
        for u in range(1, UNITS):
            unit_logits(u)
            rows(W_UV + u - 1, G_UV + (u - 1) // 2 * 2)
            unit_values(u - 1)
            unit_transpose(u)
        rows(W_GA + 1, G_GA)
        unit_values(UNITS - 1)
        rows(W_GA + 2, G_GA + 2)
        rows(W_GA + 3, G_GA + 2)
        w = weights(W_ATT, D)
        eng.wait_ge(att_hi, 1)
        eng.wait_ge(att_ready, 1)
        for k in range(4):
            n, r = k // TB, slice(k % TB * P, (k % TB + 1) * P)
            for c in range(2):
                last = three(bank(3 + k), (a_hi[:, c, r], a_lo[:, c, r]),
                             [v[:, c, n * BLKN:(n + 1) * BLKN] for v in w], c == 0, c == 1)
            last.then_inc(y_done if k < 3 else piece_done, 1)
        rows(W_GB, G_GB)
        rows(W_GB + 1, G_GB)
        eng.wait_ge(ws_ready, 1)
        eng.wait_ge(vn_ready, TB)
        eng.wait_ge(y_read, 4)
        for g in range(GMG):
            last = eng.matmul(bank(3, 3)[:, g * P:(g + 1) * P], wsT[:, g, :],
                              uv[:, :, GM + g * HD:GM + (g + 1) * HD], start=True, stop=True)
        last.then_inc(mixed_done, 1)
        rows(W_GB + 2, G_GB + 2)
        for b in range(TB):
            eng.wait_ge(g_ready, b + 1)
            eng.wait_ge(mixed_read, TB)
            for c in range(6):
                last = eng.transpose(bank(3, 3)[:, c * T + b * P:c * T + (b + 1) * P],
                                     uv[:, b, GM + c * P:GM + (c + 1) * P], ident)
        last.then_inc(gT_done, 1)
        rows(W_GB + 3, G_GB + 2)
        eng.wait_ge(gT_hi, 3)
        eng.wait_ge(gT_ready, 3)
        for j in range(3):
            w = weights(W_GM + j, D)
            for k in range(4):
                b, n = k // NB, k % NB
                r = slice(b * P, (b + 1) * P)
                for c in range(2):
                    last = three(bank(4 + k), (g_hi[:, 2 * j + c, r], g_lo[:, 2 * j + c, r]),
                                 [v[:, c, n * BLKN:(n + 1) * BLKN] for v in w], j == c == 0, j == 2 and c == 1)
                if j == 2 and k < 3:
                    last.then_inc(y_done, 1)
            last.then_inc(piece_done, 1)

        def merged_transposed(b):
            eng.wait_ge(merged_ready, NB * (b + 1))
            for c in range(KC):
                last = eng.transpose(bank(2 * b, 2)[:, c * P:(c + 1) * P], xn[:, b, c::KC], ident)
            last.then_inc(mT_done, 1)

        def mixers_out(j, b):
            w = weights(W_WO + j, D)
            for n in range(NB):
                for c in range(2):
                    cc = 2 * j + c
                    last = three(bank(4 + 2 * b + n), (xh_tb[:, b, cc, :], xl_tb[:, b, cc, :]),
                                 [v[:, c, n * BLKN:(n + 1) * BLKN] for v in w], cc == 0, cc == KC - 1)
            if b == TB - 1:
                last.then_inc(piece_done, 1)
            elif j == 3:
                last.then_inc(wo_done, 1)

        eng.wait_ge(proj_free, G_GB + 4)
        for b in range(TB):
            merged_transposed(b)
            eng.wait_ge(y_read, 6 + 2 * b)
            eng.wait_ge(mT_hi, 2 * (b + 1))
            eng.wait_ge(mT_ready, 2 * (b + 1))
            mixers_out(0, b)
        for j in range(1, 4):
            for b in range(TB):
                mixers_out(j, b)

        eng.wait_ge(small_in, 96)
        eng.wait_ge(wr_ready, 1)
        for b in range(TB):
            eng.wait_ge(h_ready, b + 1)
            for c in range(KC):
                last = eng.transpose(bank(2 * b, 2)[:, c * P:(c + 1) * P], h[:, b, c::KC], ident)
            last.then_inc(xT_done, 1)
        for b in range(TB):
            eng.wait_ge(xT_ready, KC + b + 1)
            for c in range(KC):
                last = eng.matmul(bank(4 + b)[:, 0:E], xt_route[:, b, c, :], wr[:, c, :], start=c == 0,
                                  stop=c == KC - 1)
            last.then_inc(rt_done, 1)
        eng.wait_ge(mask_ready, 1)
        eng.matmul(bank(3)[:, 0:E], before, mask[:, 0, :], start=True, stop=True).then_inc(moe_free, RING)
        eng.matmul(bank(3)[:, E:2 * E], ones[:, :], mask[:, 0, :], start=True, stop=False)
        eng.matmul(bank(3)[:, E:2 * E], before, mask[:, 1, :], start=False, stop=True)
        eng.matmul(bank(3)[:, 2 * E:3 * E], ones[:, :], mask[:, 0, :], start=True, stop=False)
        eng.matmul(bank(3)[:, 2 * E:3 * E], ones[:, :], mask[:, 1, :], start=False, stop=True).then_inc(rank_done, 1)
        def gather(pair, q):
            eng.wait_ge(sel_ready, pair * 2 + 1)
            for c in range(KC):
                for b in range(TB):
                    last = eng.matmul(bank(6, 2)[:, c * P:(c + 1) * P], xn[:, b, c::KC], sel[:, q, b, :],
                                      start=b == 0, stop=b == TB - 1)
            last.then_inc(xg_done, 1)

        eng.wait_ge(xn_ready, 4)
        gather(0, 0)
        eng.wait_ge(count_ready, 1)
        n = eng.value_load(count[0:1, 0:1], min_val=PAIRS // 2, max_val=PASSES * PAIRS // 2)
        with eng.Fori(0, n) as i:
            for q in range(2):
                pair = 2 * i + q

                def arrived(m):
                    k = q * LOADS + m
                    s = ORDER[k % RING]
                    eng.wait_ge(moe_in[s], i * (16 * 2 * LOADS // RING) + 16 * (k // RING + 1))
                    return ring[:, s, :].rearrange("p (c n) -> p c n", n=2 * D if m < 2 * UPL else D)

                def both(o, x, w, cw, n0, stop):
                    for e in range(2):
                        r = slice(CAP * e, CAP * (e + 1))
                        last = eng.matmul(o[r, :], x[:, r], w[e][:, cw, n0:n0 + BLKN], start=False, stop=stop,
                                          skip_group_check=True)
                        yield last

                eng.wait_ge(comb_added, pair * 2 + 1)
                eng.wait_ge(xg_ready, pair + 1)
                for k in range(4):
                    eng.matmul(bank(k), pick[:, bass.ds((i % (PAIRS // 2)) * (2 * P) + q * P, P)],
                               bias[:, k * BLKN:(k + 1) * BLKN], start=True, stop=False, skip_group_check=True)
                for j in range(UPL):
                    w = [arrived(2 * j + e) for e in range(2)]
                    order = [(c, k) for c in range(2) for k in range(4)] if j < UPL - 1 else \
                        [(c, k) for half in range(2) for c in range(2) for k in (half, half + 2)]
                    for at, (c, k) in enumerate(order):
                        ends = j == UPL - 1 and c == 1
                        even, odd = both(bank(k), xt_tb[:, q, 2 * j + c, :], w, c, k * BLKN, ends)
                        if at == 7:
                            even.then_inc(moe_free, 1)
                            odd.then_inc(moe_free, 1)
                        elif ends and at == 3:
                            odd.then_inc(gu_half, 1)
                eng.wait_ge(comb_added, pair * 2 + 2)
                gather(pair + 1, 1 - q)
                eng.wait_ge(act_ready, pair * 2 + 2)
                for b in range(TB):
                    last = eng.transpose(bank(2)[:, b * P:(b + 1) * P], selg[:, q, b, :], ident)
                last.then_inc(sgT_done, 1)
                for s in range(2):
                    for c in range(4):
                        last = eng.transpose(bank(s)[:, c * P:(c + 1) * P], act[:, 4 * s + c::KC], ident)
                    last.then_inc(aT_done, 1)
                for k in range(NB):
                    eng.matmul(bank(4 + k), pick[:, bass.ds((i % (PAIRS // 2)) * (2 * P) + q * P, P)],
                               bias[:, 2 * D + k * BLKN:2 * D + (k + 1) * BLKN], start=True, stop=False,
                               skip_group_check=True)
                for j in range(2):
                    w = [arrived(2 * (UPL + j) + e) for e in range(2)]
                    eng.wait_ge(aT_ready, pair * 2 + (j + 1))
                    for c in range(4):
                        for k in range(NB):
                            for e in range(2):
                                r = slice(CAP * e, CAP * (e + 1))
                                last = eng.matmul(bank(4 + k)[r, :], actT[:, 4 * j + c, r],
                                                  w[e][:, c, k * BLKN:(k + 1) * BLKN], start=False,
                                                  stop=j == 1 and c == 3, skip_group_check=True)
                                if c == 3 and k == NB - 1:
                                    last.then_inc(moe_free, 1)
                eng.wait_ge(sgT_ready, pair + 1)
                eng.wait_ge(y_ready, pair + 1)
                eng.wait_ge(xg_ready, pair + 2)
                for b in (1, 0):
                    for k in range(NB):
                        last = eng.matmul(bank((2 if b else 6) + k), selgT[:, b, :], ysb[:, k * BLKN:(k + 1) * BLKN],
                                          start=True, stop=True)
                    last.then_inc(comb_done, 1)

        eng.wait_ge(ple_in[0], 16)
        wpp = ring[:, ORDER[0], 0:2 * D].rearrange("p (c n) -> p c n", c=2)

        def embed(b):
            for k in range(NB):
                for c in range(2):
                    last = eng.matmul(bank(4 + 2 * b + k), pT[:, c, b * P:(b + 1) * P],
                                      wpp[:, c, k * BLKN:(k + 1) * BLKN], start=c == 0, stop=c == 1)
            return last

        embed(0)
        for t, b in enumerate((1, 0)):
            eng.wait_ge(xn_ready, 5 + t)
            for c in range(KC):
                last = eng.transpose(bank(2 * b, 2)[:, c * P:(c + 1) * P], xn[:, b, c::KC], ident)
            last.then_inc(xT_done, 1)
        eng.wait_ge(comb_added, n * 4 + 2)
        embed(1).then_inc(pp_done, 1)
        for k in (1, 2):
            eng.wait_ge(ple_in[k], 16)
        wpg = [ring[:, ORDER[1 + k], :].rearrange("p (c n) -> p c n", n=D) for k in range(2)]
        for t, b in enumerate((1, 0)):
            eng.wait_ge(xT_ready, KC + TB + KC // 2 * (t + 1))
            eng.wait_ge(xT_ready2, KC + KC // 2 * (t + 1))
            for k in range(NB):
                for c in range(KC):
                    last = eng.matmul(bank(2 * b + k), xt_tb[:, b, c, :], wpg[c // 4][:, c % 4, k * BLKN:(k + 1) * BLKN],
                                      start=c == 0, stop=c == KC - 1)
                last.then_inc(pg_done, 1)


def constants():
    import numpy as np

    table = np.zeros((P, CONSTS), np.float32)
    table[:, IDENT:IDENT + P] = np.eye(P)
    table[:, TRIL:TRIL + P] = np.triu(np.ones((P, P)))
    table[:, BEFORE:BEFORE + P] = np.triu(np.ones((P, P)), 1)
    table[:, IOTA:IOTA + CAP] = np.arange(CAP)
    onehot = np.zeros((BUCKETS + 1, GROUPS, SKEW), np.float32)
    exact = BUCKETS // 2
    for g, (window, dilation) in enumerate(((128, 1), (512, 4), (2048, 16))):
        for u in range(SKEW):
            dist = T - 1 - u
            if dist < 0 or dist > window or dist % dilation:
                onehot[BUCKETS, g, u] = -(2.0 ** 100)
                continue
            nf = np.maximum(np.int64(dist), 1).astype(np.float32)
            large = exact + (np.log(nf / exact) / np.log(2048 / exact) * (BUCKETS - exact)).astype(np.int32)
            onehot[dist if dist < exact else min(int(large), BUCKETS - 1), g, u] = 1.0
    pick = np.zeros((3, E, PAIRS, 2, CAP), np.float32)
    for e in range(E):
        pick[:, e, e // 2, e % 2, :] = 1.0
    return {"table_const": table, "onehot_const": onehot,
            "pick_const": pick.reshape(3 * E, PAIRS * P).astype(np.uint16) * np.uint16(BF16_ONE)}


_INS = ["x", "p", "g_mix", "w_in", "rel_bias", "w_att_out", "ln_v_g", "ln_v_b", "w_spatial", "b_spatial",
        "w_gmlp_out", "w_out", "g_moe", "w_router", "b_router", "w_gate_up", "b_gate_up", "w_down", "b_down",
        "g_ple", "w_ple_gate", "w_ple_proj", "g_final"]


def kernel(**inputs):
    import numpy as _np
    import concourse.bacc as _bacc
    from concourse import mybir as _mybir
    from concourse.bass_utils import run_bass_kernel_spmd as _run

    w_in = _np.asarray(inputs["w_in"])[0].reshape(P, KC, -1)
    cuts = _np.cumsum(in_widths())[:-1]
    inputs = dict(inputs, w_in=_np.concatenate([w.reshape(P, -1) for w in _np.split(w_in, cuts, axis=2)], axis=1),
                  p=_np.asarray(inputs["p"])[0, 0].T.reshape(P, 2, T),
                  w_spatial=_np.asarray(inputs["w_spatial"])[0].transpose(2, 0, 1),
                  b_spatial=_np.asarray(inputs["b_spatial"])[0].T)
    nc = _bacc.Bacc("TRN2", target_bir_lowering=False, num_devices=1)
    arrays, aps = {}, {}
    for name, a in list({k: inputs[k] for k in _INS}.items()) + list(constants().items()):
        a = _np.ascontiguousarray(a)
        arrays[f"in_{name}"] = a
        aps[name] = nc.dram_tensor(f"in_{name}", a.shape, _mybir.dt.from_np(a.dtype), kind="ExternalInput").ap()
    out = nc.dram_tensor("out_0", (1, T, D), _mybir.dt.float32, kind="ExternalOutput").ap()
    with ExitStack() as ctx:
        build(nc, ctx, aps, out)
    r = _run(nc, [arrays], core_ids=[0])
    return r.results[0]["out_0"]
```

```python
from contextlib import ExitStack

import concourse.bass as bass
import concourse.mybir as mybir

F32 = mybir.dt.float32
F32R = mybir.dt.float32r
BF16 = mybir.dt.bfloat16
I32 = mybir.dt.int32
U32 = mybir.dt.uint32
ALU = mybir.AluOpType
ACT = mybir.ActivationFunctionType
AX = mybir.AxisListType

P = 128
D = 1024
KC = D // P
TB = 2
T = TB * P
HD = 64
SLOTS_PER_GROUP = 4
GROUPS = 3
HEADS = GROUPS * SLOTS_PER_GROUP
QKV = HEADS * HD
GM = 768
GMG = 12
UV0 = 3 * QKV
GATE0 = UV0 + 2 * GM
BLKN = 512
NB = D // BLKN
E = 32
TOP = 4
CAP = 64
PAIRS = E // 2
PASSES = T // CAP
BUCKETS = 32
SKEW = 384
EPS = 1e-6
BF16_ONE = 0x3F80
LIMIT = 7.0
ALPHA = 1.702
SLOT = 4096
RING = 8
RAW = 3
SCRATCH = 6
ORDER = [6, 7, 3, 4, 0, 1, 2, 5]
PIECE = 2048
LOADS = 12
UPL = 8
EMBED = [(1, 0, 6), (1, 1, 7), (0, 0, 1), (0, 1, 5)]
GATE_BANK = (6, 4)
IDENT, TRIL, BEFORE, IOTA, CONSTS = 0, 128, 256, 384, 448


def in_widths():
    return [BLKN] * 4 + [QKV - BLKN] + [BLKN] * 7


def build(nc, ctx, a, out):
    def sb(name, shape, dt=F32):
        return ctx.enter_context(nc.sbuf_tensor(name, shape, dt))

    def sem(name):
        return ctx.enter_context(nc.semaphore(name))

    with ExitStack() as until_moe:
        def split(name, shape):
            return until_moe.enter_context(nc.sbuf_tensor(name, shape, F32R))

        w_hi, w_lo = split("w_hi", [P, 2, PIECE]), split("w_lo", [P, 2, PIECE])
        x_hi, x_lo = split("x_hi", [P, 2 * D]), split("x_lo", [P, 2 * D])
        pg_hi, pg_lo = split("pg_hi", [P, 2, PIECE]), split("pg_lo", [P, 2, PIECE])
        until_moe.enter_context(nc.sbuf_tensor("loads", [P, SLOT], F32))
        g_hi, g_lo = split("g_hi", [P, 6, T]), split("g_lo", [P, 6, T])
        a_hi, a_lo = split("a_hi", [P, 2, T]), split("a_lo", [P, 2, T])
    ring = sb("ring", [P, RING, SLOT])
    h = sb("h", [P, TB, D])
    xn = sb("xn", [P, TB, D])
    xt = sb("xt", [P, 2 * D])
    stage = sb("stage", [P, 3 * D])
    work = sb("work", [P, 3 * D])
    late = sb("late", [P, 1536])
    bias = sb("bias", [3 * E, 3 * D], BF16)
    pick = sb("pick", [3 * E, PAIRS * P], BF16)
    emb = sb("emb", [P, TB, D])
    const = sb("const", [P, CONSTS])
    wr = sb("wr", [P, KC, E])
    rank_of = sb("rank_of", [P, TB, PASSES * E + 4])
    gate_of = sb("gate_of", [P, TB, PASSES * E + 4])
    cols = sb("cols", [P, 3, KC])
    bs = sb("bs", [P, GMG])
    ones = sb("ones", [P, P])
    tiny = sb("tiny", [P, 96])
    route = sb("route", [P, 96])
    count = sb("count", [P, 1], I32)
    top_i = sb("top_i", [P, TB, 8], U32)
    ps = ctx.enter_context(nc.psum_tensor("ps", [P, 8, BLKN], F32))

    ident = const[:, IDENT:IDENT + P]
    before = const[:, BEFORE:BEFORE + P]
    tril_t = const[:, TRIL:TRIL + P]
    iota = const[:, IOTA:IOTA + CAP]
    xh_all, xl_all = (v[:, :].rearrange("p (c t) -> p c t", c=KC) for v in (x_hi, x_lo))
    xh_tb, xl_tb = (v[:, :].rearrange("p (b c t) -> p b c t", b=TB, c=KC) for v in (x_hi, x_lo))
    xt_tb = xt[:, :].rearrange("p (b c t) -> p b c t", b=TB, c=KC)
    scratch = ring[:, SCRATCH:RING, :].rearrange("p s n -> p (s n)")
    btab = scratch[:, 0:HEADS * T].rearrange("p (h s) -> p h s", h=HEADS)
    qkT = scratch[:, 3072:6144].rearrange("p (c t) -> p c t", c=12)
    vsb = scratch[:, 6144:7680].rearrange("p (b n) -> p b n", b=TB)
    prob = stage[:, 0:1536].rearrange("p (b g s) -> p b g s", b=2, g=GROUPS)
    probT = stage[:, 1536:2304]
    gain_moe = emb[:, 0, :]
    gain_final = work[:, 0:D]
    pT = stage[:, 2560:3072].rearrange("p (c t) -> p c t", c=2)
    sig = xt[:, :].rearrange("p (b n) -> p b n", b=4)
    gated = stage[:, 2048:2560]
    ws_raw = stage[:, 0:1536].rearrange("p (g j) -> p g j", g=GMG)
    vals = stage[0:SLOTS_PER_GROUP, 1536:1536 + GROUPS * SKEW].rearrange("p (g u) -> p g u", g=GROUPS)
    xt_route = stage[:, 0:2048].rearrange("p (b c t) -> p b c t", b=TB, c=KC)
    uv = work[:, :].rearrange("p (b n) -> p b n", b=TB)
    onehot = late[0:BUCKETS + 1, 0:GROUPS * SKEW].rearrange("p (g u) -> p g u", g=GROUPS)
    wsT = late[:, :].rearrange("p (g i) -> p g i", g=GMG)
    lng, lnb = xn[:, 0, 0:GM], xn[:, 1, 0:GM]
    relb = tiny[0:BUCKETS + 1, 80:92]
    act = stage[:, 0:D]
    actT = stage[:, D:2 * D].rearrange("p (c t) -> p c t", c=KC)
    ysb = stage[:, 2 * D:3 * D]
    glu = work[:, 0:D].rearrange("p (b n) -> p b n", b=2)
    sigm = work[:, D:2 * D].rearrange("p (b n) -> p b n", b=2)
    lin = work[:, 2 * D:3 * D].rearrange("p (b n) -> p b n", b=2)
    sel = late[:, 0:512].rearrange("p (q b s) -> p q b s", q=2, b=TB)
    selg = late[:, 512:1024].rearrange("p (q b s) -> p q b s", q=2, b=TB)
    selgT = late[:, 1024:1280].rearrange("p (b t) -> p b t", b=TB)
    mean_sq, rstd = tiny[:, 0:8], tiny[:, 8:16]
    row_max, neg_max, den, rden = tiny[:, 16:24], tiny[:, 24:32], tiny[:, 32:40], tiny[:, 40:48]
    ln_sum, ln_nm, ln_ss, ln_var, ln_rstd = (tiny[:, 48 + 2 * k:50 + 2 * k] for k in range(5))
    rms_var = tiny[:, 64:72]
    half = tiny[:, 72:73]
    fullest, passes = tiny[:, 58:59], tiny[:, 59:63]
    top_v = route[:, 0:16].rearrange("p (b k) -> p b k", b=TB)
    top_e = route[:, 16:24].rearrange("p (b k) -> p b k", b=TB)
    top_s, top_r = route[:, 24:26], route[:, 26:28]
    top_g = route[:, 32:40].rearrange("p (b k) -> p b k", b=TB)
    brout = route[:, 40:72]
    logits = work[:, 0:64].rearrange("p (b e) -> p b e", b=TB)
    chosen = work[:, 64:320].rearrange("p (b k e) -> p b k e", b=TB, k=TOP)
    weighted = work[:, 320:576].rearrange("p (b k e) -> p b k e", b=TB, k=TOP)
    mask = work[:, 576:640].rearrange("p (b e) -> p b e", b=TB)
    gates = work[:, 640:704].rearrange("p (b e) -> p b e", b=TB)
    rank1 = work[:, 704:768].rearrange("p (b e) -> p b e", b=TB)

    def gate_ple(b, k):
        return stage[:, b * D + k * BLKN:b * D + (k + 1) * BLKN]

    skewed = nc.dram_tensor("skewed", [HEADS, P, SKEW], F32)

    def bank(k, n=1):
        return ps[:, k:k + n, :].rearrange("p b n -> p (b n)")

    w_out = a["w_out"][0].rearrange("(p c) n -> p c n", c=KC)
    w_gm = a["w_gmlp_out"][0].rearrange("(c p) n -> p c n", p=P)
    widths = in_widths()

    def w_in(k):
        c0 = sum(widths[:k])
        return a["w_in"][:, KC * c0:KC * (c0 + widths[k])].rearrange("p (c n) -> p c n", c=KC)

    early_views = [w_in(k) for k in range(10)]
    early_views += [a["w_att_out"][0].rearrange("(c p) n -> p c n", p=P)]
    early_views += [w_in(10), w_in(11)]
    early_views += [w_gm[:, 0:4, :], w_gm[:, 4:6, :], w_out[:, 0:4, :], w_out[:, 4:8, :]]
    early_views += [a["w_ple_proj"][0].rearrange("(p c) n -> p c n", c=2)]
    (L_QK, L_V, L_UV, L_GA, L_ATT, L_GB, L_GM, L_WO, L_PP) = (0, 3, 5, 8, 10, 11, 13, 15, 17)
    n_early = len(early_views)

    def words(k):
        return early_views[k].shape[1] * early_views[k].shape[2]

    def halves(p, w):
        k, at = pieces[p]
        if k >= L_V:
            return early_slot(k)[:, at:at + PIECE], w[:, p % 2, :]
        n = PIECE // KC
        return (early_slot(k).rearrange("p (c n) -> p c n", c=KC)[:, :, at // KC:at // KC + n],
                w[:, p % 2, :].rearrange("p (c n) -> p c n", c=KC))

    def early_slot(k):
        return ring[:, RAW + k % RAW, 0:words(k)]

    pieces = [(k, w) for k in range(L_PP) for w in range(0, words(k), PIECE)]
    first_piece = [min(i for i, (j, _) in enumerate(pieces) if j == k) for k in range(L_PP)] + [len(pieces)]
    W_V, W_UV, W_GA, W_ATT, W_GB, W_GM, W_WO = (first_piece[k] for k in (L_V, L_UV, L_GA, L_ATT, L_GB, L_GM, L_WO))

    def gate_piece(q):
        hi, lo = (pg_hi, pg_lo) if q < 2 else (w_hi, w_lo)
        at = q % 2 * PIECE
        return ring[:, ORDER[q // 2], at:at + PIECE], hi[:, q % 2, :], lo[:, q % 2, :]

    w_up = a["w_gate_up"][0].rearrange("e (p c) n -> e p (c n)", c=KC)
    w_dn = a["w_down"][0].rearrange("e (p c) n -> e p (c n)", c=KC)
    w_pg = a["w_ple_gate"][0].rearrange("(p c) n -> p (c n)", c=KC)

    x_in = [sem(f"x_in{b}") for b in range(TB)]
    const_in, bias_in, ws_in, small_in, ln_in, gmoe_in, gfin_in, rel_in, skew_out, btab_in = (
        sem(n) for n in ("const_in", "bias_in", "ws_in", "small_in", "ln_in", "gmoe_in", "gfin_in", "rel_in",
                         "skew_out", "btab_in"))
    first_in = sem("first_in")
    early_in = [sem(f"early_in{k}") for k in range(RAW)]
    hi_ready, lo_ready, piece_done = sem("hi_ready"), sem("lo_ready"), sem("piece_done")
    moe_in = [sem(f"moe_in{k}") for k in range(RING)]
    moe_free = sem("moe_free")
    ple_in = [sem(f"ple_in{k}") for k in range(2)]
    pT_in, pg_high, pg_low = sem("pT_in"), sem("pg_high"), sem("pg_low")
    dve_step, act_step = sem("dve_step"), sem("act_step")
    ones_ready, merged_ready = sem("ones_ready"), sem("merged_ready")
    bias_part, bias_rest = sem("bias_part"), sem("bias_rest")
    vals_done, vals_ready = sem("vals_done"), sem("vals_ready")
    sq_done, xn_ready, xT_done, xT_ready = sem("sq_done"), sem("xn_ready"), sem("xT_done"), sem("xT_ready")
    x_bank_done = sem("x_bank_done")
    xT_ready2 = sem("xT_ready2")
    ws_ready, wr_ready = sem("ws_ready"), sem("wr_ready")
    proj_done, proj_free = sem("proj_done"), sem("proj_free")
    qk_done, qk_read, nm_ready, exp_done, prob_ready = (
        sem(n) for n in ("qk_done", "qk_read", "nm_ready", "exp_done", "prob_ready"))
    pT_done, pT_ready, pv_done, att_hi = sem("pT_done"), sem("pT_ready"), sem("pv_done"), sem("att_hi")
    att_ready, gT_hi, mT_hi = sem("att_ready"), sem("gT_hi"), sem("mT_hi")
    gelu_done, vn_ready, mixed_done, mixed_read, g_ready, gT_done, gT_ready = (
        sem(n) for n in ("gelu_done", "vn_ready", "mixed_done", "mixed_read", "g_ready", "gT_done", "gT_ready"))
    y_done, y_read = sem("y_done"), sem("y_read")
    mT_done, mT_ready, wo_done, h_ready = sem("mT_done"), sem("mT_ready"), sem("wo_done"), sem("h_ready")
    rt_done, mask_ready, top_sub, top_exp, rank_done, count_ready = (
        sem(n) for n in ("rt_done", "mask_ready", "top_sub", "top_exp", "rank_done", "count_ready"))
    sel_ready, xg_done, xg_ready = sem("sel_ready"), sem("xg_done"), sem("xg_ready")
    gu_half, glu_ready, sig_ready, lin_ready, mix_ready, act_ready = (
        sem(n) for n in ("gu_half", "glu_ready", "sig_ready", "lin_ready", "mix_ready", "act_ready"))
    sgT_done, sgT_ready, aT_done, aT_ready = sem("sgT_done"), sem("sgT_ready"), sem("aT_done"), sem("aT_ready")
    y_ready, comb_done, comb_added = sem("y_ready"), sem("comb_done"), sem("comb_added")
    pp_done, pp_read, pg_done, pg_sig, out_ready, out_done = (
        sem(n) for n in ("pp_done", "pp_read", "pg_done", "pg_sig", "out_ready", "out_done"))
    hsum, rstd_ready, ln_sq, ln_root = sem("hsum"), sem("rstd_ready"), sem("ln_sq"), sem("ln_root")
    pool_step = sem("pool_step")

    block = ctx.enter_context(nc.Block())

    G_V, G_UV, G_GA, G_GB = 6, 10, 16, 20
    UNITS = TB * SLOTS_PER_GROUP

    def unit(u):
        return u // TB, u % TB, u % TB + 1

    def group_piece(g):
        if g < G_V:
            return g
        k = (g // 2) if g < G_GB else g // 2 + 1
        return first_piece[k + 1] - 1

    @block.sync
    def _(sp):
        xv = a["x"][0].rearrange("(b p) d -> p b d", p=P)
        for b in range(TB):
            sp.dma_start(h[:, b, :], xv[:, b, :]).then_inc(x_in[b], 16)
        for k in range(n_early):
            if k >= RAW:
                sp.wait_ge(lo_ready, first_piece[k - RAW + 1])
            dst, src = early_slot(k).rearrange("p (c n) -> p c n", c=early_views[k].shape[1]), early_views[k]
            if k == 0:
                n = PIECE // KC
                sp.dma_start(dst[:, :, 0:n], src[:, :, 0:n]).then_inc(first_in, 16)
                dst, src = dst[:, :, n:], src[:, :, n:]
            sp.dma_start(dst, src).then_inc(early_in[k % RAW], 16)
            if k == 3:
                sp.wait_ge(vals_ready, 1)
                for g in range(GROUPS):
                    sp.dma_start(skewed[g * SLOTS_PER_GROUP:(g + 1) * SLOTS_PER_GROUP, :, :],
                                 vals[:, g, :].unsqueeze(1).to_broadcast([SLOTS_PER_GROUP, P, SKEW])).then_inc(
                        skew_out, 16)
            if k == 4:
                sp.wait_ge(skew_out, 16 * GROUPS)
                sp.dma_start(btab, bass.AP(skewed, P - 1, [[SKEW - 1, P], [P * SKEW, HEADS], [1, T]])).then_inc(
                    btab_in, 16)

        def moe_load(s, m, expert_pair):
            w, at = (w_up, m) if m < UPL else (w_dn, m - UPL)
            src = w[bass.ds(2 * expert_pair, 2), :, at * (SLOT // 2):(at + 1) * (SLOT // 2)]
            sp.dma_start(ring[:, s, :].rearrange("p (e n) -> p e n", e=2),
                         src.rearrange("e p n -> p e n")).then_inc(moe_in[s], 16)

        for k in range(2 * LOADS):
            s = ORDER[k % RING]
            if k < RING:
                if s == RAW + L_PP % RAW:
                    sp.wait_ge(pp_done, 4)
                elif RAW <= s < SCRATCH:
                    last = max(n for n in range(n_early) if n % RAW == s - RAW)
                    sp.wait_ge(lo_ready, first_piece[last + 1])
                elif s >= SCRATCH:
                    sp.wait_ge(piece_done, W_WO)
                else:
                    sp.wait_ge(piece_done, len(pieces))
            else:
                sp.wait_ge(moe_free, k + 1)
            moe_load(s, k % LOADS, k // LOADS)
        sp.wait_ge(count_ready, 1)
        n = sp.value_load(count[0:1, 0:1], min_val=PAIRS // 2, max_val=PASSES * PAIRS // 2)
        with sp.Fori(1, n) as i:
            for k in range(2 * LOADS):
                s = ORDER[k % RING]
                sp.wait_ge(moe_free, i * (2 * LOADS) + (k + 1))
                moe_load(s, k % LOADS, 2 * (i % (PAIRS // 2)) + k // LOADS)
        for k in range(2):
            sp.wait_ge(moe_free, n * (2 * LOADS) + (k + 1))
            sp.dma_start(ring[:, ORDER[k], :], w_pg[:, k * SLOT:(k + 1) * SLOT]).then_inc(ple_in[k], 16)
        ov = out[0].rearrange("(b p) d -> b p d", p=P)
        for t, b in enumerate((1, 0)):
            for k in range(NB):
                part = slice(k * BLKN, (k + 1) * BLKN)
                sp.wait_ge(out_ready, NB * t + k + 1)
                sp.dma_start(ov[b][:, part], xn[:, b, part]).then_inc(out_done, 16)
        sp.wait_ge(out_done, 16 * TB * NB)

    @block.gpsimd
    def _(pool):
        steps = [0]

        def link(ins):
            steps[0] += 1
            ins.then_inc(pool_step, 1)
            pool.wait_ge(pool_step, steps[0])

        def root(ready, got, var, src, dst, scale, done):
            pool.wait_ge(ready, got)
            link(pool.tensor_scalar(var, src, scale, EPS, ALU.mult, ALU.add))
            pool.tensor_tensor(dst, var, half, ALU.pow).then_inc(done, 1)

        def rms_root(k):
            root(sq_done, k + 1, rms_var[:, k:k + 1], mean_sq[:, k:k + 1], rstd[:, k:k + 1], 1.0, rstd_ready)

        link(pool.memset(half, -0.5))
        for k in range(TB):
            rms_root(k)
        pool.wait_ge(piece_done, 1)
        pool.dma_start(gain_moe, a["g_moe"][0].partition_broadcast(P)).then_inc(gmoe_in, 16)
        pool.dma_start(wr[:, :, :], a["w_router"][0].rearrange("(p c) e -> p c e", c=KC)).then_inc(small_in, 16)
        pool.dma_start(brout, a["b_router"][0].partition_broadcast(P)).then_inc(small_in, 16)
        pool.dma_start(cols[:, 1, :], a["g_ple"][0].rearrange("(p c) -> p c", c=KC)).then_inc(small_in, 16)
        pool.dma_start(cols[:, 2, :], a["g_moe"][0].rearrange("(p c) -> p c", c=KC)).then_inc(small_in, 16)
        pool.dma_start(pick[:, :].bitcast(mybir.dt.uint16), a["pick_const"]).then_inc(small_in, 16)
        pool.wait_ge(x_bank_done, KC // 2)
        pool.dma_start(lng, a["ln_v_g"][0].partition_broadcast(P)).then_inc(ln_in, 16)
        pool.dma_start(lnb, a["ln_v_b"][0].partition_broadcast(P)).then_inc(ln_in, 16)
        for k, rows in enumerate((slice(0, 2 * E), slice(0, E))):
            pool.wait_ge(bias_part, k + 1)
            pool.tensor_tensor(work[rows, :], work[rows, :], bias[rows, :], ALU.subtract).then_inc(bias_rest, 1)
        pool.wait_ge(small_in, 80)
        pool.tensor_tensor(wr[:, :, :], wr[:, :, :], cols[:, 2, :].unsqueeze(2).to_broadcast([P, KC, E]),
                           ALU.mult).then_inc(wr_ready, 1)
        pool.wait_ge(skew_out, 16 * GROUPS)
        pool.dma_start(pT, a["p"]).then_inc(pT_in, 16)
        for b in range(TB):
            root(ln_sq, b + 1, ln_var[:, b:b + 1], ln_ss[:, b:b + 1], ln_rstd[:, b:b + 1], 1.0 / GM, ln_root)
        for k in range(2, 4):
            rms_root(k)
        for k in range(4, 6):
            rms_root(k)
        pool.dma_start(gain_final, a["g_final"].partition_broadcast(P)).then_inc(gfin_in, 16)
        for k in range(6, 8):
            rms_root(k)

    @block.scalar
    def _(eng):
        steps = [0]

        def link(ins):
            steps[0] += 1
            ins.then_inc(act_step, 1)
            eng.wait_ge(act_step, steps[0])

        eng.dma_start(const[:, :], a["table_const"]).then_inc(const_in, 16)
        eng.dma_start(cols[:, 0, :], a["g_mix"][0].rearrange("(p c) -> p c", c=KC)).then_inc(const_in, 16)
        eng.dma_start(onehot, a["onehot_const"]).then_inc(rel_in, 16)
        eng.dma_start(relb[0:BUCKETS, :], a["rel_bias"]).then_inc(rel_in, 16)

        def mean_square(k, src, junk):
            eng.activation(junk, src, ACT.Square, scale=D ** -0.5, accum_out=mean_sq[:, k:k + 1]).then_inc(sq_done, 1)

        for b in range(TB):
            eng.wait_ge(x_in[b], 16)
            mean_square(b, h[:, b, :], xn[:, b, :])

        def high(p):
            k, w = pieces[p]
            if p == 0:
                eng.wait_ge(first_in, 16)
            elif w == 0 or p == 1:
                eng.wait_ge(early_in[k % RAW], 16 * (k // RAW + 1))
            if p >= 2:
                eng.wait_ge(piece_done, p - 1)
            raw, hi = halves(p, w_hi)
            eng.activation(hi, raw, ACT.Copy).then_inc(hi_ready, 1)

        def evac(g, dst, n, func=ACT.Copy):
            if g >= G_V and g % 2 == 0:
                eng.wait_ge(proj_done, (g - G_V) // 2 + 1)
            else:
                eng.wait_ge(piece_done, group_piece(g) + 1)
            eng.activation(dst, bank(g % 3)[:, 0:n], func).then_inc(proj_free, 1)

        high(0)
        eng.wait_ge(const_in, 32)
        for c in range(KC):
            eng.wait_ge(x_bank_done, c // 2 + 1)
            eng.activation(xh_all[:, c, :], bank(c // 2)[:, c % 2 * T:(c % 2 + 1) * T], ACT.Identity,
                           scale=cols[:, 0, c:c + 1]).then_inc(xT_ready, 1)
        high(1)
        for k in range(3):
            eng.dma_start(work[E * k:E * (k + 1), 0:2 * D], a["b_gate_up"][0]).then_inc(bias_in, 16)
            eng.dma_start(work[E * k:E * (k + 1), 2 * D:], a["b_down"][0]).then_inc(bias_in, 16)
        eng.dma_start(ws_raw, a["w_spatial"]).then_inc(ws_in, 16)
        eng.dma_start(bs[:, :], a["b_spatial"]).then_inc(ws_in, 16)

        def bias_high(k):
            if k:
                eng.wait_ge(bias_rest, k)
            else:
                eng.wait_ge(bias_in, 96)
            rows = slice(0, (3 - k) * E)
            eng.activation(bias[rows, :], work[rows, :], ACT.Copy).then_inc(bias_part, 1)

        for g in range(G_V):
            evac(g, qkT[:, 2 * g:2 * g + 2, :].rearrange("p c t -> p (c t)"), BLKN)
            high(g + 2)
            if g in (2, 4):
                bias_high(g // 2 - 1)

        def exponentials(u):
            nk = unit(u)[2] * P
            eng.wait_ge(nm_ready, u + 1)
            eng.activation(prob[:, u % 2, :, 0:nk], prob[:, u % 2, :, 0:nk], ACT.Exp, bias=neg_max[:, u:u + 1],
                           accum_out=den[:, u:u + 1]).then_inc(exp_done, 1)

        def weights_out(u):
            nk = unit(u)[2] * P
            eng.wait_ge(pT_done, u + 1)
            if u:
                eng.wait_ge(pv_done, u)
            else:
                eng.wait_ge(skew_out, 16 * GROUPS)
            eng.activation(probT[:, 0:3 * nk], bank(5, 2)[:, 0:3 * nk], ACT.Copy).then_inc(pT_ready, 1)

        high(W_V + 2)
        exponentials(0)
        bias_high(2)
        evac(G_V, vsb[:, 0, 0:BLKN], BLKN)
        evac(G_V + 1, vsb[:, 1, 0:BLKN], BLKN)
        high(W_UV)
        for b in range(TB):
            evac(G_V + 2 + b, vsb[:, b, BLKN:], QKV - BLKN)
        weights_out(0)
        for u in range(1, UNITS):
            high(W_UV + u)
            exponentials(u)
            if u in (2, 4, 6):
                if u == 2:
                    eng.wait_ge(bias_part, 3)
                for b in range(TB):
                    c0 = (u // 2 - 1) * BLKN
                    evac(G_UV + u - 2 + b, uv[:, b, c0:c0 + BLKN], BLKN)
            weights_out(u)
        high(W_GA + 2)
        evac(G_GA, sig[:, 0, :], BLKN, ACT.Sigmoid)
        evac(G_GA + 1, sig[:, 1, :], BLKN, ACT.Sigmoid)
        high(W_GA + 3)
        eng.wait_ge(proj_free, G_GA)
        for b in range(TB):
            eng.activation(uv[:, b, GM:], uv[:, b, GM:], ACT.Gelu, accum_out=ln_sum[:, b:b + 1]).then_inc(gelu_done, 1)
        eng.wait_ge(pv_done, UNITS)
        eng.activation(a_hi[:, :, :].rearrange("p c t -> p (c t)"), bank(7), ACT.Copy).then_inc(att_hi, 1)
        high(W_ATT)
        for b in range(TB):
            eng.activation(uv[:, b, 0:GM], uv[:, b, 0:GM], ACT.Gelu).then_inc(gelu_done, 1)
        evac(G_GA + 2, sig[:, 2, :], BLKN, ACT.Sigmoid)
        evac(G_GA + 3, sig[:, 3, :], BLKN, ACT.Sigmoid)
        for p in range(3):
            high(W_GB + p)
        for k in range(2):
            eng.wait_ge(y_read, k + 1)
            evac(G_GB + k, sig[:, k, :], BLKN, ACT.Sigmoid)
        high(W_GB + 3)
        high(W_GM)
        eng.wait_ge(gT_done, 1)
        for k in range(3):
            eng.activation(g_hi[:, 2 * k:2 * k + 2, :].rearrange("p c t -> p (c t)"), bank(3 + k), ACT.Copy).then_inc(
                gT_hi, 1)
        for k in (2, 3):
            eng.wait_ge(y_read, k + 1)
            evac(G_GB + k, sig[:, k, :], BLKN, ACT.Sigmoid)
        high(W_GM + 1)
        high(W_GM + 2)
        high(W_WO)
        for b in range(TB):
            eng.wait_ge(mT_done, b + 1)
            for k in range(2):
                eng.activation(xh_tb[:, b, 4 * k:4 * k + 4, :].rearrange("p c t -> p (c t)"), bank(2 * b + k),
                               ACT.Copy).then_inc(mT_hi, 1)
            if b == 0:
                high(W_WO + 1)
        high(W_WO + 2)
        high(W_WO + 3)

        for b in range(TB):
            if b == 0:
                eng.wait_ge(h_ready, 1)
                mean_square(2, h[:, 0, :], xn[:, 0, :])
            eng.wait_ge(xT_done, 1 + b)
            eng.activation(xt_route[:, b, :, :].rearrange("p c t -> p (c t)"), bank(2 * b, 2), ACT.Copy).then_inc(
                xT_ready, 1)
        eng.wait_ge(h_ready, 2)
        mean_square(3, h[:, 1, :], xn[:, 1, :])

        def embedded(i):
            b, k, o = EMBED[i]
            eng.wait_ge(pp_done, i + 1)
            if i == 2:
                eng.wait_ge(xn_ready, 4)
            eng.activation(emb[:, b, k * BLKN:(k + 1) * BLKN], bank(o), ACT.Copy).then_inc(pp_read, 1)

        embedded(0)
        eng.wait_ge(top_sub, TB)
        eng.activation(top_e, top_e, ACT.Exp).then_inc(top_exp, 1)
        embedded(1)
        embedded(2)

        def gathered(pair, q):
            eng.wait_ge(xg_done, pair + 1)
            eng.activation(xt_tb[:, q, :, :].rearrange("p c t -> p (c t)"), bank(6, 2), ACT.Copy).then_inc(xg_ready, 1)

        embedded(3)
        gathered(0, 0)
        eng.wait_ge(count_ready, 1)
        n = eng.value_load(count[0:1, 0:1], min_val=PAIRS // 2, max_val=PASSES * PAIRS // 2)
        with eng.Fori(0, n) as i:
            for q in range(2):
                pair = 2 * i + q
                for s in range(2):
                    eng.wait_ge(glu_ready, pair * 2 + (s + 1))
                    eng.activation(sigm[:, s, :], glu[:, s, :], ACT.Sigmoid, scale=ALPHA).then_inc(sig_ready, 1)
                gathered(pair + 1, 1 - q)
                eng.wait_ge(sgT_done, pair + 1)
                eng.activation(selgT.rearrange("p b t -> p (b t)"), bank(2)[:, 0:T], ACT.Copy).then_inc(sgT_ready, 1)
                for s in range(2):
                    eng.wait_ge(aT_done, pair * 2 + (s + 1))
                    eng.activation(actT[:, 4 * s:4 * s + 4, :].rearrange("p c t -> p (c t)"), bank(s),
                                   ACT.Copy).then_inc(aT_ready, 1)
                eng.wait_ge(moe_free, pair * LOADS + (RING + LOADS))
                eng.activation(ysb, bank(4, 2), ACT.Copy).then_inc(y_ready, 1)
        def gate_high(q):
            raw, hi, _ = gate_piece(q)
            eng.wait_ge(ple_in[q // 2], 16)
            eng.wait_ge(moe_free, n * (2 * LOADS) + (4 if q < 2 else 6))
            eng.activation(hi, raw, ACT.Copy).then_inc(pg_high, 1)

        def gate_tokens(t, b):
            eng.wait_ge(xT_done, 3 + t)
            for c in range(KC):
                eng.activation(xh_tb[:, b, c, :], bank(2 * b + c // 4)[:, (c % 4) * P:(c % 4 + 1) * P], ACT.Identity,
                               scale=cols[:, 1, c:c + 1]).then_inc(xT_ready, 1)

        gate_high(0)
        gate_high(1)
        gate_tokens(0, 1)
        gate_high(2)
        gate_high(3)
        gate_tokens(1, 0)
        for t, b in enumerate((1, 0)):
            eng.wait_ge(comb_added, n * 4 + (1 + t))
            mean_square(4 + t, h[:, b, :], xn[:, b, :])
        for t, b in enumerate((1, 0)):
            eng.wait_ge(rstd_ready, 5 + t)
            for k in range(NB):
                eng.wait_ge(pg_done, NB * t + k + 1)
                eng.activation(gate_ple(b, k), bank(GATE_BANK[b] + k), ACT.Sigmoid,
                               scale=rstd[:, 4 + t:5 + t]).then_inc(pg_sig, 1)
            eng.wait_ge(hsum, NB * (t + 1))
            mean_square(6 + t, h[:, b, :], xn[:, b, :])

    @block.vector
    def _(eng):
        steps = [0]

        def link(ins):
            steps[0] += 1
            ins.then_inc(dve_step, 1)
            eng.wait_ge(dve_step, steps[0])

        def normalise(k, dst, src, by=None):
            eng.wait_ge(rstd_ready, k + 1)
            if by is None:
                return eng.tensor_scalar(dst, src, rstd[:, k:k + 1], None, ALU.mult)
            return eng.scalar_tensor_tensor(out=dst, in0=src, scalar=rstd[:, k:k + 1], in1=by, op0=ALU.mult,
                                            op1=ALU.mult)

        link(eng.memset(relb[BUCKETS:BUCKETS + 1, :], 1.0))
        eng.memset(ones[:, :], 1.0).then_inc(ones_ready, 1)
        for b in range(TB):
            normalise(b, xn[:, b, :], h[:, b, :]).then_inc(xn_ready, 1)

        def low(p):
            eng.wait_ge(hi_ready, p + 1)
            if p >= 2:
                eng.wait_ge(piece_done, p - 1)
            (raw, lo), (_, hi) = halves(p, w_lo), halves(p, w_hi)
            eng.tensor_tensor(lo, raw, hi.bitcast(F32), ALU.subtract).then_inc(lo_ready, 1)

        low(0)
        for c in range(KC):
            if c % 2 == 0:
                eng.wait_ge(xT_ready, c + 2)
            eng.scalar_tensor_tensor(out=xl_all[:, c, :], in0=bank(c // 2)[:, c % 2 * T:(c % 2 + 1) * T],
                                     scalar=cols[:, 0, c:c + 1], in1=xh_all[:, c, :].bitcast(F32), op0=ALU.mult,
                                     op1=ALU.subtract).then_inc(xT_ready2, 1)
        low(1)
        low(2)
        eng.wait_ge(vals_done, 1)
        eng.tensor_copy(vals, ps[0:SLOTS_PER_GROUP, 4:7, 0:SKEW]).then_inc(vals_ready, 1)
        for p in range(3, W_V):
            low(p)
        eng.wait_ge(ws_in, 32)
        eng.tensor_tensor(wsT, ws_raw, tril_t.unsqueeze(1).to_broadcast([P, GMG, P]), ALU.mult).then_inc(ws_ready, 1)
        low(W_V)

        def scores(u):
            s, b, kb = unit(u)
            nk, off, w = kb * P, (TB - kb) * P, prob[:, u % 2, :, 0:kb * P]
            eng.wait_ge(qk_done, u + 1)
            if u >= 2:
                eng.wait_ge(pT_done, u - 1)
            eng.scalar_tensor_tensor(out=w, in0=bank(3, 2)[:, 0:3 * T].rearrange("p (g s) -> p g s", g=GROUPS)[
                :, :, 0:nk], scalar=HD ** -0.5, in1=btab[:, s::SLOTS_PER_GROUP, off:off + nk], op0=ALU.mult,
                op1=ALU.add).then_inc(qk_read, 1)
            eng.wait_ge(qk_read, u + 1)
            link(eng.tensor_reduce(row_max[:, u:u + 1], w, AX.XY, ALU.max))
            eng.tensor_scalar(neg_max[:, u:u + 1], row_max[:, u:u + 1], -1.0, None, ALU.mult).then_inc(nm_ready, 1)

        def over_sum(u):
            w = prob[:, u % 2, :, 0:unit(u)[2] * P]
            eng.wait_ge(exp_done, u + 1)
            link(eng.reciprocal(rden[:, u:u + 1], den[:, u:u + 1]))
            eng.tensor_scalar(w, w, rden[:, u:u + 1], None, ALU.mult).then_inc(prob_ready, 1)

        low(W_V + 1)
        eng.wait_ge(btab_in, 16)
        eng.wait_ge(ws_ready, 1)
        scores(0)
        over_sum(0)
        low(W_V + 2)
        low(W_UV)
        for u in range(1, UNITS):
            scores(u)
            low(W_UV + u)
            over_sum(u)
        low(W_GA + 2)
        def centre(b):
            v = uv[:, b, GM:]
            eng.wait_ge(gelu_done, b + 1)
            link(eng.tensor_scalar(ln_nm[:, b:b + 1], ln_sum[:, b:b + 1], -1.0 / GM, None, ALU.mult))
            link(eng.tensor_scalar(v, v, ln_nm[:, b:b + 1], None, ALU.add))
            eng.tensor_tensor_reduce(stage[:, 0:GM], v, v, 1.0, 0.0, ALU.mult, ALU.add,
                                     ln_ss[:, b:b + 1]).then_inc(ln_sq, 1)

        def scale(b):
            v = uv[:, b, GM:]
            eng.wait_ge(ln_root, b + 1)
            link(eng.scalar_tensor_tensor(out=v, in0=v, scalar=ln_rstd[:, b:b + 1], in1=lng, op0=ALU.mult,
                                          op1=ALU.mult))
            eng.tensor_tensor(v, v, lnb, ALU.add).then_inc(vn_ready, 1)

        def attention_out(k):
            n, b = k // TB, k % TB
            eng.wait_ge(proj_free, G_GA + k + 1)
            y_wait(0, k, W_ATT + 1)
            eng.tensor_tensor(xn[:, b, n * BLKN:(n + 1) * BLKN], bank(3 + k), sig[:, k, :],
                              ALU.mult).then_inc(y_read, 1)

        def y_wait(before_these, k, pieces_then):
            if k < 3:
                eng.wait_ge(y_done, before_these + k + 1)
            else:
                eng.wait_ge(piece_done, pieces_then)

        eng.wait_ge(ln_in, 32)
        eng.wait_ge(pT_done, UNITS)
        low(W_GA + 3)
        centre(0)
        eng.wait_ge(att_hi, 1)
        eng.tensor_tensor(a_lo[:, :, :].rearrange("p c t -> p (c t)"), bank(7),
                          a_hi[:, :, :].rearrange("p c t -> p (c t)").bitcast(F32), ALU.subtract).then_inc(att_ready, 1)
        low(W_ATT)
        scale(0)
        centre(1)
        low(W_GB)
        scale(1)
        eng.wait_ge(vn_ready, TB)
        attention_out(0)
        attention_out(1)
        low(W_GB + 1)
        attention_out(2)
        attention_out(3)
        low(W_GB + 2)
        eng.wait_ge(mixed_done, 1)
        eng.wait_ge(gelu_done, 4)
        for b in range(TB):
            v = uv[:, b, GM:].rearrange("p (g d) -> p g d", g=GMG)
            mixed = bank(3, 3).rearrange("p (g b d) -> p g b d", g=GMG, b=TB)[:, :, b, :]
            eng.tensor_tensor(v, mixed, bs[:, :].unsqueeze(2).to_broadcast([P, GMG, HD]), ALU.add).then_inc(
                mixed_read, 1)
            eng.wait_ge(mixed_read, b + 1)
            eng.tensor_tensor(uv[:, b, GM:], uv[:, b, GM:], uv[:, b, 0:GM], ALU.mult).then_inc(g_ready, 1)
        low(W_GB + 3)
        low(W_GM)
        for k in range(3):
            eng.wait_ge(gT_hi, k + 1)
            eng.tensor_tensor(g_lo[:, 2 * k:2 * k + 2, :].rearrange("p c t -> p (c t)"), bank(3 + k),
                              g_hi[:, 2 * k:2 * k + 2, :].rearrange("p c t -> p (c t)").bitcast(F32),
                              ALU.subtract).then_inc(gT_ready, 1)
        low(W_GM + 1)
        low(W_GM + 2)

        def merge(k):
            b, n = k // NB, k % NB
            m = xn[:, b, n * BLKN:(n + 1) * BLKN]
            eng.wait_ge(proj_free, G_GB + 4)
            y_wait(3, k, W_WO)
            eng.tensor_tensor(gated, bank(4 + k), sig[:, TB * n + b, :], ALU.mult).then_inc(y_read, 1)
            eng.wait_ge(y_read, 4 + k + 1)
            eng.tensor_tensor(m, m, gated, ALU.add).then_inc(merged_ready, 1)
            eng.wait_ge(merged_ready, k + 1)

        def merged_low(b):
            for k in range(2):
                eng.wait_ge(mT_hi, 2 * b + k + 1)
                eng.tensor_tensor(xl_tb[:, b, 4 * k:4 * k + 4, :].rearrange("p c t -> p (c t)"), bank(2 * b + k),
                                  xh_tb[:, b, 4 * k:4 * k + 4, :].rearrange("p c t -> p (c t)").bitcast(F32),
                                  ALU.subtract).then_inc(mT_ready, 1)

        for b in range(TB):
            merge(NB * b)
            merge(NB * b + 1)
            if b == 0:
                low(W_WO)
            merged_low(b)
        low(W_WO + 1)
        low(W_WO + 2)
        low(W_WO + 3)
        for b in range(TB):
            eng.wait_ge(*((piece_done, len(pieces)) if b else (wo_done, 1)))
            eng.tensor_tensor(h[:, b, :], h[:, b, :], bank(4 + 2 * b, 2), ALU.add).then_inc(h_ready, 1)
        eng.wait_ge(gmoe_in, 16)

        eng.wait_ge(small_in, 80)
        for b in range(TB):
            eng.wait_ge(h_ready, b + 1)
            normalise(2 + b, xn[:, b, :], h[:, b, :], gain_moe).then_inc(xn_ready, 1)
            eng.wait_ge(rt_done, b + 1)
            link(eng.scalar_tensor_tensor(out=logits[:, b, :], in0=bank(4 + b)[:, 0:E], scalar=rstd[:, 2 + b:3 + b],
                                          in1=brout, op0=ALU.mult, op1=ALU.add))
            link(eng.max(top_v[:, b, :], logits[:, b, :]))
            link(eng.max_index(top_i[:, b, :], top_v[:, b, :], logits[:, b, :]))
            link(eng.tensor_tensor(chosen[:, b, :, :], iota[:, 0:E].unsqueeze(1).to_broadcast([P, TOP, E]),
                                   top_i[:, b, 0:TOP].unsqueeze(2).to_broadcast([P, TOP, E]), ALU.is_equal))
            link(eng.tensor_reduce(mask[:, b, :], chosen[:, b, :, :].rearrange("p k e -> p e k"), AX.X, ALU.add))
            if b == 1:
                eng.memset(rank_of[:, :, PASSES * E:], -1.0).then_inc(mask_ready, 1)
            eng.tensor_scalar(top_e[:, b, :], top_v[:, b, 0:TOP], top_v[:, b, 0:1], None, ALU.subtract).then_inc(
                top_sub, 1)
        eng.wait_ge(top_exp, 1)
        link(eng.tensor_reduce(top_s, top_e, AX.X, ALU.add))
        link(eng.reciprocal(top_r, top_s))
        link(eng.tensor_tensor(top_g, top_e, top_r.unsqueeze(2).to_broadcast([P, TB, TOP]), ALU.mult))
        for b in range(TB):
            link(eng.tensor_tensor(weighted[:, b, :, :], chosen[:, b, :, :],
                                   top_g[:, b, :].unsqueeze(2).to_broadcast([P, TOP, E]), ALU.mult))
        link(eng.tensor_reduce(gates, weighted.rearrange("p b k e -> p b e k"), AX.X, ALU.add))
        for r in range(PASSES):
            steps[0] += 1
            eng.tensor_copy(gate_of[:, :, r * E:(r + 1) * E], gates).then_inc(dve_step, 1)
        eng.memset(gate_of[:, :, PASSES * E:], 0.0).then_inc(comb_added, 2)
        eng.wait_ge(dve_step, steps[0])
        eng.wait_ge(comb_added, 2)
        eng.wait_ge(mask_ready, 1)
        eng.wait_ge(rank_done, 1)
        ranks = bank(3)[:, 0:2 * E].rearrange("p (b e) -> p b e", b=TB)
        link(eng.scalar_tensor_tensor(out=rank1, in0=ranks, scalar=1.0, in1=mask, op0=ALU.add, op1=ALU.mult))
        for r in range(PASSES):
            steps[0] += 1
            eng.tensor_scalar(rank_of[:, :, r * E:(r + 1) * E], rank1, -1.0 - CAP * r, None, ALU.add).then_inc(
                dve_step, 1)
        eng.wait_ge(dve_step, steps[0])

        def select(pair, q):
            r2 = rank_of[:, :, bass.ds(pair * 2, 2)].unsqueeze(3).to_broadcast([P, TB, 2, CAP])
            g2 = gate_of[:, :, bass.ds(pair * 2, 2)].unsqueeze(3).to_broadcast([P, TB, 2, CAP])
            io = iota.unsqueeze(1).unsqueeze(1).to_broadcast([P, TB, 2, CAP])
            s4 = sel[:, q, :, :].rearrange("p b (e s) -> p b e s", e=2)
            g4 = selg[:, q, :, :].rearrange("p b (e s) -> p b e s", e=2)
            eng.tensor_tensor(s4, io, r2, ALU.is_equal).then_inc(sel_ready, 1)
            eng.wait_ge(sel_ready, pair * 2 + 1)
            eng.tensor_tensor(g4, s4, g2, ALU.mult).then_inc(sel_ready, 1)

        select(0, 0)
        link(eng.tensor_reduce(fullest, bank(3)[:, 2 * E:3 * E], AX.X, ALU.max))
        for r in range(1, PASSES):
            link(eng.tensor_scalar(passes[:, r:r + 1], fullest, float(CAP * r), PAIRS / 2, ALU.is_gt, ALU.mult))
        link(eng.tensor_reduce(passes[:, 0:1], passes[:, 1:PASSES], AX.X, ALU.add))
        eng.tensor_scalar(count[:, :], passes[:, 0:1], PAIRS / 2, None, ALU.add).then_inc(count_ready, 1)
        eng.wait_ge(count_ready, 1)
        n = eng.value_load(count[0:1, 0:1], min_val=PAIRS // 2, max_val=PASSES * PAIRS // 2)
        with eng.Fori(0, n) as i:
            for q in range(2):
                pair = 2 * i + q
                select(pair + 1, 1 - q)
                for s in range(2):
                    k = pair * 2 + (s + 1)
                    if s == 0:
                        eng.wait_ge(gu_half, pair + 1)
                    else:
                        eng.wait_ge(moe_free, pair * LOADS + (RING + UPL))
                    eng.tensor_scalar(glu[:, s, :], bank(s), LIMIT, None, ALU.min).then_inc(glu_ready, 1)
                    eng.tensor_scalar(lin[:, s, :], bank(2 + s), LIMIT, -LIMIT, ALU.min, ALU.max).then_inc(
                        lin_ready, 1)
                    eng.wait_ge(glu_ready, k)
                    eng.wait_ge(lin_ready, k)
                    eng.scalar_tensor_tensor(out=lin[:, s, :], in0=lin[:, s, :], scalar=1.0, in1=glu[:, s, :],
                                             op0=ALU.add, op1=ALU.mult).then_inc(mix_ready, 1)
                    eng.wait_ge(mix_ready, k)
                    eng.wait_ge(sig_ready, k)
                    eng.tensor_tensor(act[:, s * BLKN:(s + 1) * BLKN], lin[:, s, :], sigm[:, s, :],
                                      ALU.mult).then_inc(act_ready, 1)
                for b in (1, 0):
                    eng.wait_ge(comb_done, pair * 2 + (2 - b))
                    eng.wait_ge(comb_added, pair * 2 + (3 - b))
                    eng.tensor_tensor(h[:, b, :], h[:, b, :], bank(2 if b else 6, 2), ALU.add).then_inc(
                        comb_added, 1)
        eng.wait_ge(comb_added, n * 4 + 2)
        def gate_low(q):
            raw, hi, lo = gate_piece(q)
            eng.wait_ge(pg_high, q + 1)
            eng.tensor_tensor(lo, raw, hi.bitcast(F32), ALU.subtract).then_inc(pg_low, 1)

        def gate_tokens_low(t, b, first):
            eng.wait_ge(xT_ready, KC + TB + KC * t + first + 4)
            for c in range(first, first + 4):
                eng.scalar_tensor_tensor(out=xl_tb[:, b, c, :], in0=bank(2 * b + c // 4)[:, (c % 4) * P:(c % 4 + 1) * P],
                                         scalar=cols[:, 1, c:c + 1], in1=xh_tb[:, b, c, :].bitcast(F32), op0=ALU.mult,
                                         op1=ALU.subtract).then_inc(xT_ready2, 1)

        gate_low(0)
        gate_tokens_low(0, 1, 0)
        gate_low(1)
        gate_tokens_low(0, 1, 4)
        gate_low(2)
        gate_low(3)
        gate_tokens_low(1, 0, 0)
        gate_tokens_low(1, 0, 4)
        eng.wait_ge(pp_read, 4)
        eng.wait_ge(gfin_in, 16)
        for t, b in enumerate((1, 0)):
            for k in range(NB):
                part = h[:, b, k * BLKN:(k + 1) * BLKN]
                eng.wait_ge(pg_sig, NB * t + k + 1)
                link(eng.tensor_tensor(gate_ple(b, k), gate_ple(b, k), emb[:, b, k * BLKN:(k + 1) * BLKN], ALU.mult))
                eng.tensor_tensor(part, part, gate_ple(b, k), ALU.add).then_inc(hsum, 1)
            for k in range(NB):
                part = slice(k * BLKN, (k + 1) * BLKN)
                normalise(6 + t, xn[:, b, part], h[:, b, part], gain_final[:, part]).then_inc(out_ready, 1)

    @block.tensor
    def _(eng):
        def three(o, a, b, first, last):
            eng.matmul(o, a[0], b[0], start=first, stop=False)
            eng.matmul(o, a[1], b[0], start=False, stop=False)
            return eng.matmul(o, a[0], b[1], start=False, stop=last)

        def weights(p, n):
            eng.wait_ge(hi_ready, p + 1)
            eng.wait_ge(lo_ready, p + 1)
            return [v[:, p % 2, :].rearrange("p (c n) -> p c n", n=n) for v in (w_hi, w_lo)]

        eng.wait_ge(const_in, 32)
        for b in range(TB):
            eng.wait_ge(xn_ready, b + 1)
            for c in range(KC):
                last = eng.transpose(bank(c // 2)[:, c % 2 * T + b * P:c % 2 * T + (b + 1) * P], xn[:, b, c::KC], ident)
                if b == TB - 1 and c % 2:
                    last.then_inc(x_bank_done, 1)

        def group(g):
            if g >= 3:
                eng.wait_ge(proj_free, g - 2)
            elif g:
                eng.wait_ge(xT_ready2, 2 * g + 2)
            return bank(g % 3)

        def relative_bias():
            eng.wait_ge(rel_in, 32)
            eng.wait_ge(ones_ready, 1)
            for g in range(GROUPS):
                last = eng.matmul(bank(4 + g)[0:SLOTS_PER_GROUP, 0:SKEW],
                                  relb[:, g * SLOTS_PER_GROUP:(g + 1) * SLOTS_PER_GROUP], onehot[:, g, :], start=True,
                                  stop=True)
            last.then_inc(vals_done, 1)

        def features(p):
            w, o = weights(p, PIECE // KC), group(p)
            for f in range(2):
                for c in range(KC):
                    if p == 0 and f == 0:
                        eng.wait_ge(xT_ready, c + 1)
                        eng.wait_ge(xT_ready2, max(c + 1, 2))
                    last = three(o[:, f * T:(f + 1) * T], [v[:, c, f * P:(f + 1) * P] for v in w],
                                 (xh_all[:, c, :], xl_all[:, c, :]), c == 0, c == KC - 1)
            last.then_inc(piece_done, 1)

        def rows(p, g, n=BLKN):
            w, per = weights(p, n), PIECE // n
            c0 = 0 if per == KC else (p - first_piece[pieces[p][0]]) * per
            for b in range(TB):
                o = group(g + b)[:, 0:n]
                for c in range(per):
                    r = slice(b * P, (b + 1) * P)
                    last = three(o, (xh_all[:, c0 + c, r], xl_all[:, c0 + c, r]), [v[:, c, :] for v in w],
                                 c0 + c == 0, c0 + c == KC - 1)
                if b == 0 and c0 + per == KC:
                    last.then_inc(proj_done, 1)
            last.then_inc(piece_done, 1)

        def unit_logits(u):
            s, b, kb = unit(u)
            eng.wait_ge(proj_free, G_V)
            eng.wait_ge(vals_ready, 1)
            if u:
                eng.wait_ge(qk_read, u)
            for g in range(GROUPS):
                hd = g * SLOTS_PER_GROUP + s
                r = slice(HD * (hd % 2), HD * (hd % 2 + 1))
                last = eng.matmul(bank(3, 2)[:, g * T:g * T + kb * P], qkT[r, hd // 2, b * P:(b + 1) * P],
                                  qkT[r, 6 + hd // 2, 0:kb * P], start=True, stop=True)
            last.then_inc(qk_done, 1)

        def unit_transpose(u):
            s, b, kb = unit(u)
            eng.wait_ge(prob_ready, u + 1)
            if u:
                eng.wait_ge(pT_ready, u)
            for g in range(GROUPS):
                for k in range(kb):
                    o = (g * kb + k) * P
                    last = eng.transpose(bank(5, 2)[:, o:o + P], prob[:, u % 2, g, k * P:(k + 1) * P], ident)
            last.then_inc(pT_done, 1)

        def unit_values(u):
            s, b, kb = unit(u)
            eng.wait_ge(pT_ready, u + 1)
            eng.wait_ge(proj_free, G_UV)
            o = bank(7)[HD * (s % 2):HD * (s % 2 + 1), s // 2 * T + b * P:s // 2 * T + (b + 1) * P]
            for g in range(GROUPS):
                for k in range(kb):
                    hd, t = g * SLOTS_PER_GROUP + s, (g * kb + k) * P
                    last = eng.matmul(o, vsb[:, k, hd * HD:(hd + 1) * HD], probT[:, t:t + P],
                                      start=g == 0 and k == 0, stop=g == GROUPS - 1 and k == kb - 1)
            last.then_inc(pv_done, 1)

        for p in range(W_V):
            features(p)
            if p == 0:
                relative_bias()
        rows(W_V, G_V)
        unit_logits(0)
        rows(W_V + 1, G_V)
        rows(W_V + 2, G_V + 2, QKV - BLKN)
        unit_transpose(0)
        for u in range(1, UNITS):
            unit_logits(u)
            rows(W_UV + u - 1, G_UV + (u - 1) // 2 * 2)
            unit_values(u - 1)
            unit_transpose(u)
        rows(W_GA + 1, G_GA)
        unit_values(UNITS - 1)
        rows(W_GA + 2, G_GA + 2)
        rows(W_GA + 3, G_GA + 2)
        w = weights(W_ATT, D)
        eng.wait_ge(att_hi, 1)
        eng.wait_ge(att_ready, 1)
        for k in range(4):
            n, r = k // TB, slice(k % TB * P, (k % TB + 1) * P)
            for c in range(2):
                last = three(bank(3 + k), (a_hi[:, c, r], a_lo[:, c, r]),
                             [v[:, c, n * BLKN:(n + 1) * BLKN] for v in w], c == 0, c == 1)
            last.then_inc(y_done if k < 3 else piece_done, 1)
        rows(W_GB, G_GB)
        rows(W_GB + 1, G_GB)
        eng.wait_ge(ws_ready, 1)
        eng.wait_ge(vn_ready, TB)
        eng.wait_ge(y_read, 4)
        for g in range(GMG):
            last = eng.matmul(bank(3, 3)[:, g * P:(g + 1) * P], wsT[:, g, :],
                              uv[:, :, GM + g * HD:GM + (g + 1) * HD], start=True, stop=True)
        last.then_inc(mixed_done, 1)
        rows(W_GB + 2, G_GB + 2)
        for b in range(TB):
            eng.wait_ge(g_ready, b + 1)
            eng.wait_ge(mixed_read, TB)
            for c in range(6):
                last = eng.transpose(bank(3, 3)[:, c * T + b * P:c * T + (b + 1) * P],
                                     uv[:, b, GM + c * P:GM + (c + 1) * P], ident)
        last.then_inc(gT_done, 1)
        rows(W_GB + 3, G_GB + 2)
        eng.wait_ge(gT_hi, 3)
        eng.wait_ge(gT_ready, 3)
        for j in range(3):
            w = weights(W_GM + j, D)
            for k in range(4):
                b, n = k // NB, k % NB
                r = slice(b * P, (b + 1) * P)
                for c in range(2):
                    last = three(bank(4 + k), (g_hi[:, 2 * j + c, r], g_lo[:, 2 * j + c, r]),
                                 [v[:, c, n * BLKN:(n + 1) * BLKN] for v in w], j == c == 0, j == 2 and c == 1)
                if j == 2 and k < 3:
                    last.then_inc(y_done, 1)
            last.then_inc(piece_done, 1)

        def merged_transposed(b):
            eng.wait_ge(merged_ready, NB * (b + 1))
            for c in range(KC):
                last = eng.transpose(bank(2 * b, 2)[:, c * P:(c + 1) * P], xn[:, b, c::KC], ident)
            last.then_inc(mT_done, 1)

        def mixers_out(j, b):
            w = weights(W_WO + j, D)
            for n in range(NB):
                for c in range(2):
                    cc = 2 * j + c
                    last = three(bank(4 + 2 * b + n), (xh_tb[:, b, cc, :], xl_tb[:, b, cc, :]),
                                 [v[:, c, n * BLKN:(n + 1) * BLKN] for v in w], cc == 0, cc == KC - 1)
            if b == TB - 1:
                last.then_inc(piece_done, 1)
            elif j == 3:
                last.then_inc(wo_done, 1)

        eng.wait_ge(proj_free, G_GB + 4)
        for b in range(TB):
            merged_transposed(b)
            eng.wait_ge(y_read, 6 + 2 * b)
            eng.wait_ge(mT_hi, 2 * b + 1)
            eng.wait_ge(mT_ready, 2 * b + 1)
            mixers_out(0, b)
        for j in range(1, 4):
            if j == 1:
                eng.wait_ge(mT_hi, 4)
                eng.wait_ge(mT_ready, 4)
            for b in range(TB):
                mixers_out(j, b)

        eng.wait_ge(small_in, 80)
        eng.wait_ge(wr_ready, 1)
        for b in range(TB):
            eng.wait_ge(h_ready, b + 1)
            for c in range(KC):
                last = eng.transpose(bank(2 * b, 2)[:, c * P:(c + 1) * P], h[:, b, c::KC], ident)
            last.then_inc(xT_done, 1)
        for b in range(TB):
            eng.wait_ge(xT_ready, KC + b + 1)
            for c in range(KC):
                last = eng.matmul(bank(4 + b)[:, 0:E], xt_route[:, b, c, :], wr[:, c, :], start=c == 0,
                                  stop=c == KC - 1)
            last.then_inc(rt_done, 1)
        eng.wait_ge(early_in[L_PP % RAW], 16 * (L_PP // RAW + 1))
        eng.wait_ge(pT_in, 16)
        wpp = early_slot(L_PP).rearrange("p (c n) -> p c n", c=2)

        def embed(i):
            b, k, o = EMBED[i]
            for c in range(2):
                last = eng.matmul(bank(o), pT[:, c, b * P:(b + 1) * P], wpp[:, c, k * BLKN:(k + 1) * BLKN],
                                  start=c == 0, stop=c == 1)
            last.then_inc(pp_done, 1)

        embed(0)
        embed(1)
        eng.wait_ge(mask_ready, 1)
        eng.matmul(bank(3)[:, 0:E], before, mask[:, 0, :], start=True, stop=True).then_inc(moe_free, RING)
        eng.matmul(bank(3)[:, E:2 * E], ones[:, :], mask[:, 0, :], start=True, stop=False)
        eng.matmul(bank(3)[:, E:2 * E], before, mask[:, 1, :], start=False, stop=True)
        eng.matmul(bank(3)[:, 2 * E:3 * E], ones[:, :], mask[:, 0, :], start=True, stop=False)
        eng.matmul(bank(3)[:, 2 * E:3 * E], ones[:, :], mask[:, 1, :], start=False, stop=True).then_inc(rank_done, 1)
        def gather(pair, q):
            eng.wait_ge(sel_ready, pair * 2 + 1)
            for c in range(KC):
                for b in range(TB):
                    last = eng.matmul(bank(6, 2)[:, c * P:(c + 1) * P], xn[:, b, c::KC], sel[:, q, b, :],
                                      start=b == 0, stop=b == TB - 1)
            last.then_inc(xg_done, 1)

        embed(2)
        embed(3)
        eng.wait_ge(xn_ready, 4)
        eng.wait_ge(pp_read, 2)
        gather(0, 0)
        eng.wait_ge(count_ready, 1)
        n = eng.value_load(count[0:1, 0:1], min_val=PAIRS // 2, max_val=PASSES * PAIRS // 2)
        with eng.Fori(0, n) as i:
            for q in range(2):
                pair = 2 * i + q

                def arrived(m):
                    k = q * LOADS + m
                    s = ORDER[k % RING]
                    eng.wait_ge(moe_in[s], i * (16 * 2 * LOADS // RING) + 16 * (k // RING + 1))
                    return ring[:, s, :].rearrange("p (e c n) -> p e c n", e=2, n=2 * D if m < UPL else D)

                def both(o, x, w, cw, n0, stop):
                    for e in range(2):
                        r = slice(CAP * e, CAP * (e + 1))
                        last = eng.matmul(o[r, :], x[:, r], w[:, e, cw, n0:n0 + BLKN], start=False, stop=stop,
                                          skip_group_check=True)
                    return last

                eng.wait_ge(comb_added, pair * 2 + 1)
                eng.wait_ge(xg_ready, pair + 1)
                for k in range(4):
                    eng.matmul(bank(k), pick[:, bass.ds((i % (PAIRS // 2)) * (2 * P) + q * P, P)],
                               bias[:, k * BLKN:(k + 1) * BLKN], start=True, stop=False, skip_group_check=True)
                for c in range(KC):
                    w = arrived(c)
                    for k in (0, 2, 1, 3):
                        last = both(bank(k), xt_tb[:, q, c, :], w, 0, k * BLKN, c == KC - 1)
                        if c == KC - 1 and k == 2:
                            last.then_inc(gu_half, 1)
                    last.then_inc(moe_free, 1)
                eng.wait_ge(comb_added, pair * 2 + 2)
                gather(pair + 1, 1 - q)
                eng.wait_ge(act_ready, pair * 2 + 2)
                for b in range(TB):
                    last = eng.transpose(bank(2)[:, b * P:(b + 1) * P], selg[:, q, b, :], ident)
                last.then_inc(sgT_done, 1)
                for s in range(2):
                    for c in range(4):
                        last = eng.transpose(bank(s)[:, c * P:(c + 1) * P], act[:, 4 * s + c::KC], ident)
                    last.then_inc(aT_done, 1)
                for k in range(NB):
                    eng.matmul(bank(4 + k), pick[:, bass.ds((i % (PAIRS // 2)) * (2 * P) + q * P, P)],
                               bias[:, 2 * D + k * BLKN:2 * D + (k + 1) * BLKN], start=True, stop=False,
                               skip_group_check=True)
                for j in range(LOADS - UPL):
                    w = arrived(UPL + j)
                    eng.wait_ge(aT_ready, pair * 2 + (j // 2 + 1))
                    for c in range(2):
                        for k in range(NB):
                            last = both(bank(4 + k), actT[:, 2 * j + c, :], w, c, k * BLKN, j == 3 and c == 1)
                    last.then_inc(moe_free, 1)
                eng.wait_ge(sgT_ready, pair + 1)
                eng.wait_ge(y_ready, pair + 1)
                eng.wait_ge(xg_ready, pair + 2)
                for b in (1, 0):
                    for k in range(NB):
                        last = eng.matmul(bank((2 if b else 6) + k), selgT[:, b, :], ysb[:, k * BLKN:(k + 1) * BLKN],
                                          start=True, stop=True)
                    last.then_inc(comb_done, 1)

        for t, b in enumerate((1, 0)):
            eng.wait_ge(comb_added, n * 4 + 1 + t)
            for c in range(KC):
                last = eng.transpose(bank(2 * b, 2)[:, c * P:(c + 1) * P], h[:, b, c::KC], ident)
            last.then_inc(xT_done, 1)

        def gated_by(b, c, k):
            _, hi, lo = gate_piece(c // 2)
            at = (c % 2) * D + k * BLKN
            return three(bank(GATE_BANK[b] + k), (xh_tb[:, b, c, :], xl_tb[:, b, c, :]),
                         (hi[:, at:at + BLKN], lo[:, at:at + BLKN]), c == 0, c == KC - 1)

        for c in range(KC):
            eng.wait_ge(xT_ready2, KC + c + 1)
            eng.wait_ge(pg_high, c // 2 + 1)
            eng.wait_ge(pg_low, c // 2 + 1)
            for k in range(NB):
                last = gated_by(1, c, k)
                if c == KC - 1:
                    last.then_inc(pg_done, 1)
        eng.wait_ge(xT_ready2, 3 * KC)
        for k in range(NB):
            for c in range(KC):
                last = gated_by(0, c, k)
            last.then_inc(pg_done, 1)


def constants():
    import numpy as np

    table = np.zeros((P, CONSTS), np.float32)
    table[:, IDENT:IDENT + P] = np.eye(P)
    table[:, TRIL:TRIL + P] = np.triu(np.ones((P, P)))
    table[:, BEFORE:BEFORE + P] = np.triu(np.ones((P, P)), 1)
    table[:, IOTA:IOTA + CAP] = np.arange(CAP)
    onehot = np.zeros((BUCKETS + 1, GROUPS, SKEW), np.float32)
    exact = BUCKETS // 2
    for g, (window, dilation) in enumerate(((128, 1), (512, 4), (2048, 16))):
        for u in range(SKEW):
            dist = T - 1 - u
            if dist < 0 or dist > window or dist % dilation:
                onehot[BUCKETS, g, u] = -(2.0 ** 100)
                continue
            nf = np.maximum(np.int64(dist), 1).astype(np.float32)
            large = exact + (np.log(nf / exact) / np.log(2048 / exact) * (BUCKETS - exact)).astype(np.int32)
            onehot[dist if dist < exact else min(int(large), BUCKETS - 1), g, u] = 1.0
    pick = np.zeros((3, E, PAIRS, 2, CAP), np.float32)
    for e in range(E):
        pick[:, e, e // 2, e % 2, :] = 1.0
    return {"table_const": table, "onehot_const": onehot,
            "pick_const": pick.reshape(3 * E, PAIRS * P).astype(np.uint16) * np.uint16(BF16_ONE)}


_INS = ["x", "p", "g_mix", "w_in", "rel_bias", "w_att_out", "ln_v_g", "ln_v_b", "w_spatial", "b_spatial",
        "w_gmlp_out", "w_out", "g_moe", "w_router", "b_router", "w_gate_up", "b_gate_up", "w_down", "b_down",
        "g_ple", "w_ple_gate", "w_ple_proj", "g_final"]


def kernel(**inputs):
    import numpy as _np
    import concourse.bacc as _bacc
    from concourse import mybir as _mybir
    from concourse.bass_utils import run_bass_kernel_spmd as _run

    w_in = _np.asarray(inputs["w_in"])[0].reshape(P, KC, -1)
    cuts = _np.cumsum(in_widths())[:-1]
    inputs = dict(inputs, w_in=_np.concatenate([w.reshape(P, -1) for w in _np.split(w_in, cuts, axis=2)], axis=1),
                  p=_np.asarray(inputs["p"])[0, 0].T.reshape(P, 2, T),
                  w_spatial=_np.asarray(inputs["w_spatial"])[0].transpose(2, 0, 1),
                  b_spatial=_np.asarray(inputs["b_spatial"])[0].T)
    nc = _bacc.Bacc("TRN2", target_bir_lowering=False, num_devices=1)
    arrays, aps = {}, {}
    for name, a in list({k: inputs[k] for k in _INS}.items()) + list(constants().items()):
        a = _np.ascontiguousarray(a)
        arrays[f"in_{name}"] = a
        aps[name] = nc.dram_tensor(f"in_{name}", a.shape, _mybir.dt.from_np(a.dtype), kind="ExternalInput").ap()
    out = nc.dram_tensor("out_0", (1, T, D), _mybir.dt.float32, kind="ExternalOutput").ap()
    with ExitStack() as ctx:
        build(nc, ctx, aps, out)
    r = _run(nc, [arrays], core_ids=[0])
    return r.results[0]["out_0"]
```
